# Optimizing a Trainium2 kernel written in Bass

```python
import jax, jax.numpy as jnp
from jax import lax
import numpy as np

D_MODEL = 1024
BATCH = 1
SEQ = 256
DEPTH = 2

CONV_CH = 512
CONV_K = 3
GLA_HEADS = 4
GLA_DK = 64
GLA_DV = 128
GLA_KW = GLA_HEADS * GLA_DK
GLA_VW = GLA_HEADS * GLA_DV
GLA_RANK = 16
GLA_TAU = 16.0
GLA_CHUNK = 64
N_BRANCH = 2
IN_SIZES = (CONV_CH, CONV_CH, CONV_CH, GLA_KW, GLA_KW, GLA_VW, GLA_VW, GLA_RANK, D_MODEL, D_MODEL)
IN_COLS = 3 * CONV_CH + 2 * GLA_KW + 2 * GLA_VW + GLA_RANK + 2 * D_MODEL
D_FF = 2816
N_EXPERTS = 8
TOP_K = 2
D_FF_EXPERT = 3584
N_DENSE = (DEPTH + 1) // 2
N_MOE = DEPTH // 2
EPS = 1e-6

kernel_name = "hybrid_conv_gla_moe_block"

def rmsnorm(x, g):
    xf = x.astype(jnp.float32)
    y = xf * lax.rsqrt(jnp.mean(xf * xf, axis=-1, keepdims=True) + EPS)
    return (y * g.astype(jnp.float32)).astype(x.dtype)

def short_conv(u, w):
    c = u.shape[-1]
    return lax.conv_general_dilated(u, w.astype(u.dtype)[:, None, :], window_strides=(1,),
                                    padding=[(CONV_K - 1, 0)],
                                    dimension_numbers=("NWC", "WIO", "NWC"),
                                    feature_group_count=c)

def gla(q, k, v, log_a):
    bn, t, h, dk = q.shape
    dv = v.shape[-1]
    L = GLA_CHUNK
    n = t // L

    def to_chunks(z):
        return z.astype(jnp.float32).reshape(bn, n, L, h, z.shape[-1]).transpose(1, 0, 3, 2, 4)

    qc, kc, vc, gc = (to_chunks(z) for z in (q * (dk ** -0.5), k, v, log_a))
    causal = jnp.tril(jnp.ones((L, L), dtype=bool))

    def step(S, inp):
        q_, k_, v_, g_ = inp
        b = jnp.cumsum(g_, axis=-2)
        o_inter = jnp.einsum("bhlk,bhkv->bhlv", q_ * jnp.exp(b), S)
        diff = b[:, :, :, None, :] - b[:, :, None, :, :]
        decay = jnp.exp(jnp.where(causal[:, :, None], diff, -jnp.inf))
        scores = jnp.einsum("bhik,bhjk,bhijk->bhij", q_, k_, decay)
        o = o_inter + jnp.einsum("bhij,bhjv->bhiv", scores, v_)
        b_last = b[:, :, -1:, :]
        S = jnp.exp(b_last[:, :, 0, :])[..., None] * S + jnp.einsum(
            "bhjk,bhjv->bhkv", k_ * jnp.exp(b_last - b), v_)
        return S, o

    S0 = jnp.zeros((bn, h, dk, dv), jnp.float32)
    _, o = lax.scan(step, S0, (qc, kc, vc, gc))
    return o.transpose(1, 0, 3, 2, 4).reshape(bn, t, h, dv)

def token_mixer(hn, w_in, w_a2, b_a, conv_w, gla_norm_g, w_branch, w_out):
    bn, t, _ = hn.shape
    p = hn @ w_in
    idx, acc = [], 0
    for s in IN_SIZES[:-1]:
        acc += s
        idx.append(acc)
    xc, gb_c, gc_c, q, k, v, g_out, a_low, gate_a, gate_b = jnp.split(p, idx, axis=-1)
    y_a = gb_c * short_conv(gc_c * xc, conv_w)
    log_a = jax.nn.log_sigmoid((a_low @ w_a2 + b_a).astype(jnp.float32)) / GLA_TAU
    o = gla(q.reshape(bn, t, GLA_HEADS, GLA_DK), k.reshape(bn, t, GLA_HEADS, GLA_DK),
            v.reshape(bn, t, GLA_HEADS, GLA_DV), log_a.reshape(bn, t, GLA_HEADS, GLA_DK))
    o = rmsnorm(o, gla_norm_g).astype(hn.dtype).reshape(bn, t, GLA_VW)
    y_b = o * jax.nn.silu(g_out)
    ya_d = y_a @ w_branch[0]
    yb_d = y_b @ w_branch[1]
    merged = jax.nn.sigmoid(gate_a) * ya_d + jax.nn.sigmoid(gate_b) * yb_d
    return merged @ w_out

def swiglu(h, w_gate, w_up, w_down):
    return (jax.nn.silu(h @ w_gate) * (h @ w_up)) @ w_down

def moe(h, w_router, w_gate, w_up, w_down):
    logits = (h @ w_router).astype(jnp.float32)
    top_l, top_i = lax.top_k(logits, TOP_K)
    top_w = jax.nn.softmax(top_l, axis=-1)
    gates = jnp.sum(jax.nn.one_hot(top_i, N_EXPERTS, dtype=jnp.float32) * top_w[..., None],
                    axis=-2).astype(h.dtype)
    y = jnp.zeros_like(h)
    for e in range(N_EXPERTS):
        y = y + gates[..., e:e + 1] * swiglu(h, w_gate[e], w_up[e], w_down[e])
    return y

def setup_inputs(seed: int = 0) -> dict:
    key = jax.random.key(seed)
    ks = jax.random.split(key, 24)
    f32 = jnp.float32

    def nrm(k, shape, fan_in):
        return jax.random.normal(k, shape, f32) * (fan_in ** -0.5)

    def gain(k, shape):
        return 1.0 + 0.02 * jax.random.normal(k, shape, f32)

    return {
        "x": jax.random.normal(ks[0], (BATCH, SEQ, D_MODEL), f32),
        "ln1_g": gain(ks[1], (DEPTH, D_MODEL)),
        "w_in": nrm(ks[2], (DEPTH, D_MODEL, IN_COLS), D_MODEL),
        "w_a2": nrm(ks[3], (DEPTH, GLA_RANK, GLA_KW), GLA_RANK),
        "b_a": 0.1 * jax.random.normal(ks[4], (DEPTH, GLA_KW), f32),
        "conv_w": nrm(ks[5], (DEPTH, CONV_K, CONV_CH), CONV_K),
        "gla_norm_g": gain(ks[6], (DEPTH, GLA_DV)),
        "w_branch": nrm(ks[7], (DEPTH, N_BRANCH, CONV_CH, D_MODEL), CONV_CH),
        "w_out": nrm(ks[8], (DEPTH, D_MODEL, D_MODEL), D_MODEL),
        "ln2_g": gain(ks[9], (DEPTH, D_MODEL)),
        "ffn_w_gate": nrm(ks[10], (N_DENSE, D_MODEL, D_FF), D_MODEL),
        "ffn_w_up": nrm(ks[11], (N_DENSE, D_MODEL, D_FF), D_MODEL),
        "ffn_w_down": nrm(ks[12], (N_DENSE, D_FF, D_MODEL), D_FF),
        "w_router": nrm(ks[13], (N_MOE, D_MODEL, N_EXPERTS), D_MODEL),
        "moe_w_gate": nrm(ks[14], (N_MOE, N_EXPERTS, D_MODEL, D_FF_EXPERT), D_MODEL),
        "moe_w_up": nrm(ks[15], (N_MOE, N_EXPERTS, D_MODEL, D_FF_EXPERT), D_MODEL),
        "moe_w_down": nrm(ks[16], (N_MOE, N_EXPERTS, D_FF_EXPERT, D_MODEL), D_FF_EXPERT),
        "final_g": gain(ks[17], (D_MODEL,)),
    }

def reference(x, ln1_g, w_in, w_a2, b_a, conv_w, gla_norm_g, w_branch, w_out, ln2_g,
              ffn_w_gate, ffn_w_up, ffn_w_down, w_router, moe_w_gate, moe_w_up, moe_w_down,
              final_g):
    for l in range(DEPTH):
        x = x + token_mixer(rmsnorm(x, ln1_g[l]), w_in[l], w_a2[l], b_a[l], conv_w[l],
                            gla_norm_g[l], w_branch[l], w_out[l])
        h = rmsnorm(x, ln2_g[l])
        j = l // 2
        if l % 2 == 0:
            x = x + swiglu(h, ffn_w_gate[j], ffn_w_up[j], ffn_w_down[j])
        else:
            x = x + moe(h, w_router[j], moe_w_gate[j], moe_w_up[j], moe_w_down[j])
    return rmsnorm(x, final_g)


_drawn_inputs = setup_inputs


def setup_inputs(seed=0):
    import zlib

    import numpy as np

    out = dict(_drawn_inputs(seed))
    spreads = {}
    factors = {}
    for name, (base, spread) in spreads.items():
        noise = np.random.default_rng([zlib.crc32(name.encode()), seed]).standard_normal(out[name].shape)
        drawn = base * np.exp(spread * noise) if base else spread * noise
        out[name] = __import__('jax').numpy.asarray(drawn.astype(out[name].dtype))
    for name, factor in factors.items():
        out[name] = (out[name] * factor).astype(out[name].dtype)
    return out
```

```python
from contextlib import ExitStack

import numpy as np

import concourse.bass as bass
from concourse import mybir

F32 = mybir.dt.float32
F32R = mybir.dt.float32r
I32 = mybir.dt.int32
ALU = mybir.AluOpType
ACT = mybir.ActivationFunctionType
AX = mybir.AxisListType

P = 128
D = 1024
SEQ = 256
TB = SEQ // P
KT = D // P
DEPTH = 2
CONV = 512
CB = CONV // P
TAPS = 3
HEADS = 4
DK = 64
DV = 128
KW = HEADS * DK
VW = HEADS * DV
HP = HEADS // 2
RANK = 16
TAU = 16.0
L = 64
NCH = SEQ // L
FF = 2816
NE = 8
TOPK = 2
FFE = 3584
EPS = 1e-6
LEVELS = [32, 16, 8, 4, 2, 1]
NL = len(LEVELS)

CHUNK = 2048
PIECE = CHUNK // 2
R = 6
H = 4

C_X, C_GB, C_GC = 0, CONV, 2 * CONV
C_Q = 3 * CONV
C_K = C_Q + KW
C_V = C_K + KW
C_GO = C_V + VW
C_AL = C_GO + VW
C_GA = C_AL + RANK
C_GBR = C_GA + D

WIN = ([("q", C_Q), ("k", C_K), ("v0", C_V), ("v1", C_V + 256), ("xc0", C_X), ("xc1", C_X + 256),
        ("gc0", C_GC), ("gc1", C_GC + 256), ("gb0", C_GB), ("gb1", C_GB + 256),
        ("go0", C_GO), ("go1", C_GO + 256)]
       + [(f"ga{n}", C_GA + 256 * n) for n in range(4)] + [(f"gr{n}", C_GBR + 256 * n) for n in range(4)])
MIX_CHUNKS = 1 + len(WIN) + 4 + 4
MIX_PIECES = 2 * MIX_CHUNKS
UNIT_NAMES = ([f"n1{n}" for n in range(4)] + ["alow"] + [w[0] for w in WIN] + ["ya0", "ya1"]
              + ["yt0", "yt1", "ya2", "ya3"] + [f"yb{n}" for n in range(4)] + [f"wo{n}" for n in range(4)]
              + [f"n2{n}" for n in range(4)])
UNIT = {name: n for n, name in enumerate(UNIT_NAMES)}
NU = len(UNIT_NAMES)
UNIT_PIECES = {"alow": 2, **{w[0]: 4 + 2 * n for n, w in enumerate(WIN)}, "ya0": 44, "ya1": 44, "ya2": 46, "ya3": 46,
               "yb0": 48, "yb1": 48, "yb2": 50, "yb3": 50, "wo0": 56, "wo1": 56, "wo2": 58, "wo3": 58}
TURNED = {name: n + 1 for n, name in enumerate([f"n1{n}" for n in range(4)] + ["yt0", "yt1"]
                                               + [f"n2{n}" for n in range(4)])}

STEPS = FF // 256
FFN_PIECES = 6 * STEPS
ESTEPS = FFE // 512
ITEM_CHUNKS = 6 * ESTEPS
ITEM_PIECES = 2 * ITEM_CHUNKS
SLOTS = 128
EXTRA = (SEQ * TOPK) // (SLOTS + 1)
MAX_ITEMS = NE + EXTRA

MIX_BASE = [0, MIX_PIECES + FFN_PIECES]
FFN_BASE = MIX_PIECES
MOE_BASE = 2 * MIX_PIECES + FFN_PIECES
assert H == 4 and R == 6 and (ITEM_CHUNKS % R, ITEM_PIECES % H) == (0, 0)

K_ID, K_TRI, K_ONE, K_IOTA, K_RESET = 0, 128, 256, 384, 512
K_LVL = K_RESET + SEQ
K_REV = K_LVL + (NL + 1) * L
K_EID = K_REV + NE
K_PW = K_EID + NE
K_END = K_PW + HEADS


def constants():
    c = np.zeros((P, K_END), np.float32)
    a = np.arange(P)
    c[:, K_ID:K_ID + P] = a[:, None] == a[None, :]
    c[:, K_TRI:K_TRI + P] = a[:, None] < a[None, :]
    c[:, K_ONE:K_ONE + P] = 1.0
    c[:, K_IOTA:K_IOTA + P] = a[None, :] + 1
    c[:, K_RESET:K_RESET + SEQ] = (np.arange(SEQ) % L != 0)[None, :]
    j, i = (a % L)[:, None], np.arange(L)[None, :]
    for n, m in enumerate(LEVELS):
        c[:, K_LVL + n * L:K_LVL + (n + 1) * L] = (j // (2 * m) == i // (2 * m)) & (i // m % 2 == 1) & (j // m % 2 == 0)
    c[:, K_LVL + NL * L:K_LVL + (NL + 1) * L] = j == i
    c[:, K_REV:K_REV + NE] = NE - np.arange(NE)[None, :]
    c[:, K_EID:K_EID + NE] = np.arange(NE)[None, :]
    c[:, K_PW:K_PW + HEADS] = -0.5
    return c


def trunk(nc, x_d, ln1_d, w_in_d, w_a2_d, small_d, gla_g_d, w_br_d, w_out_d, ln2_d, fg_d, fu_d, fd_d,
          w_r_d, eg_d, eu_d, ed_d, fin_d, const_d, out_d):
    with ExitStack() as ctx:
        def sb(name, shape, dt=F32):
            return ctx.enter_context(nc.sbuf_tensor(name, shape, dt))

        def sem(name):
            return ctx.enter_context(nc.semaphore(name))

        bank = [ctx.enter_context(nc.psum_tensor(f"bank{n}", [P, 512], F32)) for n in range(8)]

        raw = sb("raw", [P, R, CHUNK])
        w_hi = sb("w_hi", [P, H, PIECE], F32R)
        w_lo = sb("w_lo", [P, H, PIECE], F32R)
        const = sb("const", [P, K_END])
        x = sb("x", [P, TB, D])
        gain = sb("gain", [P, 2, D])
        xt_hi = sb("xt_hi", [P, KT, SEQ], F32R)
        xt_lo = sb("xt_lo", [P, KT, SEQ], F32R)
        area = sb("area", [P, 6144], F32R)
        ya_hi, ya_lo = (area[:, n * 1024:(n + 1) * 1024].rearrange("p (b t) -> p b t", b=CB) for n in (0, 1))
        yb_hi, yb_lo = (area[:, n * 1024:(n + 1) * 1024].rearrange("p (b t) -> p b t", b=CB) for n in (2, 3))
        fh_hi, fh_lo = (area[:, n * 1024:(n + 1) * 1024].rearrange("p (s k t) -> p s k t", s=2, k=2) for n in (0, 1))
        hn_hi, hn_lo = (area[:, n * 2048:(n + 1) * 2048].rearrange("p (b d) -> p b d", b=TB) for n in (0, 1))
        eh_hi, eh_lo = (area[:, 4096 + n * 512:4096 + (n + 1) * 512].rearrange("p (k s) -> p k s", k=4) for n in (0, 1))
        perm = area[:, 5120:5376].rearrange("p (b s) -> p b s", b=TB)
        perm_t = area[:, 5376:5632]
        ex_hi, ex_lo = (t[:, 0:4, :].rearrange("p k t -> p (k t)").rearrange("p (k s) -> p k s", k=KT)
                        for t in (xt_hi, xt_lo))
        ys_hi, ys_lo = (t[:, 4:8, :].rearrange("p k t -> p (k t)") for t in (xt_hi, xt_lo))
        zeros = sb("zeros", [P, 512], F32R)
        wr_hi = sb("wr_hi", [P, KT, NE], F32R)
        wr_lo = sb("wr_lo", [P, KT, NE], F32R)
        wr_raw = sb("wr_raw", [P, KT, NE])

        work = sb("work", [P, 17160])

        def carve(at, *shape):
            n = int(np.prod(shape))
            flat = work[:, at:at + n]
            if len(shape) == 1:
                return flat
            names = "abcd"[:len(shape)]
            spec = f"p ({' '.join(names)}) -> p {' '.join(names)}"
            return flat.rearrange(spec, **dict(zip(names, shape)))

        hn = carve(0, TB, D)
        gate = carve(0, 2, KT, SEQ)
        qT, kT = carve(4096, HP, SEQ), carve(4608, HP, SEQ)
        v = carve(5120, TB, VW)
        gs = carve(6144, TB, VW)
        qe, ke = carve(7168, NL, SEQ), carve(8704, NL, SEQ)
        yb = carve(7168, TB, VW)
        ex = carve(10240, NL + 1, SEQ)
        kdT, qiT = carve(12288, HP, SEQ), carve(12800, HP, SEQ)
        u = carve(13312, CB, SEQ + 2)
        cv = carve(14344, CB, SEQ)
        kd = carve(13312, TB, HP, P)
        st = carve(13824, NCH - 1, HP, DV)
        sc = carve(14592, TB, HEADS, L)
        bb, zz, la = carve(15368, HP, SEQ), carve(15880, HP, SEQ), carve(16392, HP, SEQ)
        eb = la
        al = carve(16904, SEQ)
        sg = carve(4096, 512)
        hf = carve(4608, 2, 512)
        rt = carve(8192, 1024)

        small = sb("small", [P, DEPTH, CB * TAPS + HP])
        wa2 = sb("wa2", [RANK, DEPTH, KW])
        glag = sb("glag", [P, DEPTH, DV])
        ss = sb("ss", [P, TB])
        rs = sb("rs", [P, TB])
        oss = sb("oss", [P, TB, HEADS])
        ors = sb("ors", [P, TB, HEADS])
        keys = sb("keys", [P, TB, MAX_ITEMS + 1])
        gates = sb("gates", [P, TB, MAX_ITEMS + 1])
        items = sb("items", [P, 1 + MAX_ITEMS], I32)

        ident = const[:, K_ID:K_ID + P]
        ones = const[:, K_ONE:K_ONE + P]

        params_in = sem("params_in")
        x_in = sem("x_in")
        gain_in = [sem("gain_in0"), sem("gain_in1")]
        raw_in = [sem(f"raw_in{n}") for n in range(R)]
        hi_done, lo_done, piece_used = sem("hi_done"), sem("lo_done"), sem("piece_used")
        turned = sem("turned")
        x_new = sem("x_new")
        sq_done, hn_done = sem("sq_done"), sem("hn_done")
        ms_done, rs_done, oms_done, ors_done = sem("ms_done"), sem("rs_done"), sem("oms_done"), sem("ors_done")
        th_done, tl_done = sem("th_done"), sem("tl_done")
        dve_step, act_step, pool_step = sem("dve_step"), sem("act_step"), sem("pool_step")
        al_done, z_full, z_read, abs_done, log_done, b_done = (sem(n) for n in (
            "al_done", "z_full", "z_read", "abs_done", "log_done", "b_done"))
        q_done, k_done, v_done, xc_done, silu_done, gate_done, gs_done = (sem(n) for n in (
            "q_done", "k_done", "v_done", "xc_done", "silu_done", "gate_done", "gs_done"))
        eb_done, expo_done, exp_done, qk_done, kd_made, qi_done = (sem(n) for n in (
            "eb_done", "expo_done", "exp_done", "qk_done", "kd_made", "qi_done"))
        kdt_full, kdt_done, inc_full, st_done, sc_full, sc_done, o_full, o_sq, yb_done = (sem(n) for n in (
            "kdt_full", "kdt_done", "inc_full", "st_done", "sc_full", "sc_done", "o_full", "o_sq", "yb_done"))
        o_part = sem("o_part")
        gc_done, pa_done, pb_done = sem("gc_done"), sem("pa_done"), sem("pb_done")
        ya_made, ya_h, ya_l, yt_h, yt_l, mg_made, mg_h, mg_l = (sem(n) for n in (
            "ya_made", "ya_h", "ya_l", "yt_h", "yt_l", "mg_made", "mg_h", "mg_l"))
        sg_done, hf_done, fh_h, fh_l = (sem(n) for n in ("sg_done", "hf_done", "fh_h", "fh_l"))
        wr_h, wr_l, hn_h, hn_l, lg_full, dif_done, pex_done, mask_done, rank_full, routed, init_done = (
            sem(n) for n in ("wr_h", "wr_l", "hn_h", "hn_l", "lg_full", "dif_done", "pex_done", "mask_done",
                             "rank_full", "routed", "init_done"))
        perm_done, gather_full, gh_done, gl_done, pt_full, pt_done = (sem(n) for n in (
            "perm_done", "gather_full", "gh_done", "gl_done", "pt_full", "pt_done"))
        esg_done, ehf_done, t_full, eh_h, eh_l = (sem(n) for n in (
            "esg_done", "ehf_done", "t_full", "eh_h", "eh_l"))
        cleared, ey_h, ey_l, scat_full, scat_done = (sem(n) for n in (
            "cleared", "ey_h", "ey_l", "scat_full", "scat_done"))
        stored = sem("stored")

        def unit_read(l, name):
            kind, n = (name, 0) if name in ("alow", "q", "k") else (name[:2], int(name[2:] or 0) if name[:1] != "v" else 0)
            if name in ("alow", "q", "k"):
                return {"alow": al_done, "q": q_done, "k": k_done}[name], l + 1
            if name[0] == "v":
                return v_done, 2 * l + int(name[1]) + 1
            if kind in ("n1", "n2"):
                return tl_done, 8 * l + 4 * (kind == "n2") + n + 1
            if kind in ("xc", "gc", "gb", "go", "yt"):
                return {"xc": xc_done, "gc": gc_done, "gb": ya_made, "go": silu_done, "yt": yt_l}[kind], 2 * l + n + 1
            if kind in ("ga", "gr"):
                return gate_done, 8 * l + 4 * (kind == "gr") + n + 1
            if kind in ("ya", "yb"):
                return {"ya": pa_done, "yb": pb_done}[kind], 4 * l + n + 1
            return x_new, 8 * l + (0, 2, 1, 3).index(n) + 1

        block = ctx.enter_context(nc.Block())

        @block.sync
        def _(sp):
            def load(c, src, wait=None):
                if wait is not None:
                    sp.wait_ge(lo_done, wait)
                elif c >= R:
                    sp.wait_ge(lo_done, 2 * (c - R) + 2)
                dst = raw[:, c % R, :].rearrange("p (k n) -> p k n", k=src.shape[1])
                sp.dma_start(dst, src).then_inc(raw_in[c % R], 16)

            def rows(w, k0, nk, c0, ncol):
                return w[k0 * P:(k0 + nk) * P, c0:c0 + ncol].rearrange("(k p) n -> p k n", p=P)

            def load_gain(n, src):
                if n >= 2:
                    sp.wait_ge(hn_done, 2 * (n - 1))
                sp.dma_start(gain[:, n % 2, :], src.partition_broadcast(P)).then_inc(gain_in[n % 2], 16)

            sp.dma_start(x[:, :, :], x_d[0].rearrange("(b p) d -> p b d", p=P)).then_inc(x_in, 16)
            load_gain(0, ln1_d[0])
            sp.dma_start(const[:, :], const_d).then_inc(params_in, 16)
            load(0, rows(w_in_d[0], 0, KT, C_AL, 256))
            sp.dma_start(small[:, :, :], small_d.rearrange("l p n -> p l n")).then_inc(params_in, 16)
            sp.dma_start(wa2[:, :, :], w_a2_d.rearrange("l r n -> r l n")).then_inc(params_in, 16)
            sp.dma_start(glag[:, :, :], gla_g_d.partition_broadcast(P)).then_inc(params_in, 16)
            sp.dma_start(wr_raw[:, :, :], w_r_d[0].rearrange("(k p) e -> p k e", p=P)).then_inc(params_in, 16)

            for l in range(DEPTH):
                c = MIX_BASE[l] // 2
                if l:
                    load(c, rows(w_in_d[l], 0, KT, C_AL, 256))
                c += 1
                for n, (_, col) in enumerate(WIN):
                    load(c + n, rows(w_in_d[l], 0, KT, col, 256))
                    if n == 12:
                        load_gain(2 * l + 1, ln2_d[l])
                c += len(WIN)
                for br in range(2):
                    for n in range(2):
                        load(c + 2 * br + n, rows(w_br_d[l, br], 0, CB, 512 * n, 512))
                c += 4
                for kh in range(2):
                    for n in range(2):
                        load(c + 2 * kh + n, rows(w_out_d[l], 4 * kh, 4, 512 * n, 512))
                if l == 0:
                    c = FFN_BASE // 2
                    load(c, rows(fg_d[0], 0, KT, 0, 256))
                    load(c + 1, rows(fu_d[0], 0, KT, 0, 256))
                    load_gain(2, ln1_d[1])
                    with sp.Fori(0, (STEPS - 1) // 2) as r:
                        for s in range(2):
                            for n in range(3):
                                cc = c + 2 + 3 * s + n
                                w = (fg_d, fu_d, fd_d)[n][0]
                                if n < 2:
                                    w = w.rearrange("(k p) (m n) -> m p k n", p=P, n=256)[bass.ds(2 * r + (s + 1), 1)]
                                else:
                                    w = w.rearrange("(m k p) n -> m p k n", p=P, k=2)[bass.ds(2 * r + s, 1)]
                                load(cc, w.rearrange("m p k n -> (m p) k n"), wait=12 * r + 2 * (cc - R) + 2)
                    load(c + 3 * STEPS - 1, rows(fd_d[0], 2 * (STEPS - 1), 2, 0, D))

            load_gain(4, fin_d)

            c = MOE_BASE // 2

            def expert(w, e, k0, nk, c0, ncol):
                w = w[0][bass.ds(e, 1)]
                return w.rearrange("m k n -> (m k) n"), k0, nk, c0, ncol

            def load_item(e, i):
                def gate_up(w, half, col):
                    w = w[0].rearrange("e (k p) n -> e p k n", p=P)[bass.ds(e, 1), :, 4 * half:4 * half + 4, col]
                    return w.rearrange("m p k n -> (m p) k n")

                def down(first):
                    w = ed_d[0].rearrange("e (k p) n -> e p k n", p=P)[bass.ds(e, 1), :, first]
                    return w.rearrange("m p k n -> (m p) k n")

                for n in range(4):
                    load(c + n, gate_up((eg_d, eu_d)[n // 2], n % 2, slice(0, 512)),
                         wait=ITEM_PIECES * i + 2 * (c + n - R) + 2)
                with sp.Fori(0, ESTEPS - 1) as r:
                    for n in range(4):
                        load(c + 4 + n, gate_up((eg_d, eu_d)[n // 2], n % 2, bass.ds(512 * r + 512, 512)),
                             wait=ITEM_PIECES * i + 12 * r + 2 * (c + 4 + n - R) + 2)
                    for n in range(2):
                        load(c + 8 + n, down(bass.ds(4 * r + 2 * n, 2)),
                             wait=ITEM_PIECES * i + 12 * r + 2 * (c + 8 + n - R) + 2)
                for n in range(2):
                    cc = c + ITEM_CHUNKS - 2 + n
                    load(cc, down(slice(4 * (ESTEPS - 1) + 2 * n, 4 * (ESTEPS - 1) + 2 * n + 2)),
                         wait=ITEM_PIECES * i + 2 * (cc - R) + 2)

            with sp.Fori(0, NE) as i:
                load_item(i, i)
            sp.wait_ge(routed, 1)
            n_items = sp.value_load(items[0:1, 0:1], min_val=NE, max_val=MAX_ITEMS)
            with sp.If(n_items > NE):
                with sp.Fori(NE, n_items) as i:
                    e = sp.value_load(items[0:1, bass.ds(i + 1, 1)], min_val=0, max_val=NE - 1)
                    load_item(e, i)

            for t in range(TB):
                sp.wait_ge(hn_done, 2 * 4 + t + 1)
                sp.dma_start(out_d[0, t * P:(t + 1) * P, :], hn[:, t, :]).then_inc(stored, 16)
            sp.wait_ge(stored, 16 * TB)

        @block.scalar
        def _(act):
            cur = [0]
            chain = [0]

            def step(ins):
                chain[0] += 1
                ins.then_inc(act_step, 1)
                act.wait_ge(act_step, chain[0])

            def split(q, turn=None, used=None):
                c = q // 2
                if q % 2 == 0:
                    act.wait_ge(raw_in[c % R], 16 * (c // R + 1) if turn is None else turn)
                if used is not None:
                    act.wait_ge(piece_used, used)
                elif q >= H:
                    act.wait_ge(piece_used, q - H + 1)
                src = raw[:, c % R, (q % 2) * PIECE:(q % 2 + 1) * PIECE]
                nc.scalar.copy(w_hi[:, q % H, :], src).then_inc(hi_done, 1)

            def until(q):
                while cur[0] < q:
                    n = cur[0]
                    split(n)
                    cur[0] += 1

            def full(l, name):
                if name in TURNED:
                    act.wait_ge(turned, len(TURNED) * l + TURNED[name])
                else:
                    act.wait_ge(piece_used, MIX_BASE[l] + UNIT_PIECES[name])
                return bank[(NU * l + UNIT[name]) % 4]

            def norm_squares(n):
                for t in range(TB):
                    if n == 0:
                        act.wait_ge(x_in, 16)
                    else:
                        act.wait_ge(x_new, x_after[n] - 2 + 2 * t if n < 4 else x_after[n])
                    nc.scalar.activation(hn[:, t, :], x[:, t, :], ACT.Square,
                                         accum_out=ss[:, t:t + 1]).then_inc(sq_done, 1)

            def norm_transposed(n):
                l, name = divmod(n, 2)
                for m in range(4):
                    src = full(l, f"n{name + 1}{m}")
                    nc.scalar.copy(xt_hi[:, 2 * m:2 * m + 2, :],
                                   src[:, :].rearrange("p (k t) -> p k t", k=2)).then_inc(th_done, 1)

            x_after = [0, 4, 8, 12, 16]

            for l in range(DEPTH):
                base = MIX_BASE[l]

                def after(chunk, base=base):
                    until(base + 2 * chunk + 2 + H)

                until(base + H)
                norm_squares(2 * l)
                norm_transposed(2 * l)
                after(1)
                src = full(l, "q")
                nc.scalar.mul(qT[:, :, :], src[:, :].rearrange("p (b t) -> p b t", b=HP), DK ** -0.5).then_inc(q_done, 1)
                after(2)
                src = full(l, "k")
                nc.scalar.copy(kT[:, :, :], src[:, :].rearrange("p (b t) -> p b t", b=HP)).then_inc(k_done, 1)
                act.wait_ge(abs_done, l + 1)
                step(nc.scalar.activation(la[:, :, :], la[:, :, :], ACT.Exp, scale=-1.0))
                nc.scalar.activation(la[:, :, :], la[:, :, :], ACT.Ln, bias=1.0).then_inc(log_done, 1)
                for n in range(2):
                    after(3 + n)
                    src = full(l, f"v{n}")
                    nc.scalar.copy(v[:, :, 256 * n:256 * n + 256],
                                   src[:, :].rearrange("p (b n) -> p b n", b=TB)).then_inc(v_done, 1)
                act.wait_ge(b_done, l + 1)
                nc.scalar.activation(eb[:, :, :], bb[:, :, :], ACT.Exp, scale=1.0 / TAU).then_inc(eb_done, 1)
                for n in range(2):
                    after(5 + n)
                    src = full(l, f"xc{n}")
                    nc.scalar.copy(cv[:, 2 * n:2 * n + 2, :],
                                   src[:, :].rearrange("p (b t) -> p b t", b=2)).then_inc(xc_done, 1)
                for h in range(HP):
                    after(7 + 3 * h)
                    act.wait_ge(expo_done, HP * l + h + 1)
                    nc.scalar.activation(ex[:, :, :], ex[:, :, :], ACT.Exp, scale=1.0 / TAU).then_inc(exp_done, 1)
                after(11)
                act.wait_ge(ya_made, 2 * l + 2)
                nc.scalar.copy(ya_hi[:, :, :], cv[:, :, :]).then_inc(ya_h, 1)
                for n in range(2):
                    after(11 + n)
                    src = full(l, f"go{n}")
                    nc.scalar.activation(gs[:, :, 256 * n:256 * n + 256],
                                         src[:, :].rearrange("p (b n) -> p b n", b=TB), ACT.Silu).then_inc(silu_done, 1)
                for n in range(8):
                    after(13 + n)
                    if n == 1:
                        act.wait_ge(kdt_full, l + 1)
                        nc.scalar.copy(kd[:, :, :, :], bank[7][:, :].rearrange("p (b h n) -> p b h n", b=TB, h=HP)
                                       ).then_inc(kdt_done, 1)
                    name = f"{('ga', 'gr')[n // 4]}{n % 4}"
                    src = full(l, name)
                    nc.scalar.activation(gate[:, n // 4, 2 * (n % 4):2 * (n % 4) + 2, :],
                                         src[:, :].rearrange("p (b t) -> p b t", b=2), ACT.Sigmoid).then_inc(gate_done, 1)
                for t in range(TB):
                    act.wait_ge(o_full, TB * l + t + 1)
                    for h in range(HEADS):
                        ins = nc.scalar.activation(yb[:, t, h * DV:(h + 1) * DV], bank[6 + t][:, h * DV:(h + 1) * DV],
                                                   ACT.Square, accum_out=oss[:, t, h:h + 1])
                    ins.then_inc(o_sq, 1)
                after(21)
                for n in range(2):
                    src = full(l, f"yt{n}")
                    nc.scalar.copy(yb_hi[:, 2 * n:2 * n + 2, :],
                                   src[:, :].rearrange("p (b t) -> p b t", b=2)).then_inc(yt_h, 1)
                for n in range(2):
                    after(23 + n)
                    for m in range(2):
                        act.wait_ge(mg_made, 4 * l + 2 * n + m + 1)
                        kk = 4 * n + 2 * m
                        nc.scalar.copy(xt_hi[:, kk:kk + 2, :], gate[:, 1, kk:kk + 2, :]).then_inc(mg_h, 1)
                until(base + MIX_PIECES + H)
                norm_squares(2 * l + 1)
                norm_transposed(2 * l + 1)

                if l == 0:
                    q0 = FFN_BASE
                    until(q0 + 2 + H)
                    act.wait_ge(piece_used, q0 + 2)
                    nc.scalar.activation(sg[:, :], bank[0][:, :], ACT.Silu).then_inc(sg_done, 1)
                    until(q0 + 4 + H)
                    act.wait_ge(hf_done, 1)
                    nc.scalar.copy(fh_hi[:, 0, :, :], hf[:, 0, :].rearrange("p (k t) -> p k t", k=2)).then_inc(fh_h, 1)
                    with act.Fori(0, (STEPS - 1) // 2) as r:
                        for s in range(2):
                            first = q0 + 4 + 6 * s

                            def loop_split(lo, hi, first=first):
                                for n in range(lo, hi):
                                    q = first + H + n
                                    split(q, turn=16 * r + 16 * (q // 2 // R + 1), used=12 * r + q - H + 1)
                            loop_split(0, 2)
                            act.wait_ge(piece_used, 12 * r + first + 2)
                            nc.scalar.activation(sg[:, :], bank[0][:, :], ACT.Silu).then_inc(sg_done, 1)
                            loop_split(2, 4)
                            act.wait_ge(hf_done, 2 * r + s + 2)
                            nc.scalar.copy(fh_hi[:, 1 - s, :, :],
                                           hf[:, 1 - s, :].rearrange("p (k t) -> p k t", k=2)).then_inc(fh_h, 1)
                            loop_split(4, 6)
                    cur[0] = q0 + 4 + 6 * (STEPS - 1) + H

            act.wait_ge(params_in, 80)
            nc.scalar.copy(wr_hi[:, :, :], wr_raw[:, :, :]).then_inc(wr_h, 1)
            nc.scalar.copy(hn_hi[:, :, :], hn[:, :, :]).then_inc(hn_h, 1)
            act.wait_ge(dif_done, 1)
            nc.scalar.activation(rt[:, 64:66], rt[:, 66:68], ACT.Exp).then_inc(pex_done, 1)
            def gather_copies(count):
                for m in range(2):
                    act.wait_ge(gather_full, count + m)
                    nc.scalar.copy(ex_hi[:, 4 * m:4 * m + 4, :],
                                   bank[6 + m][:, :].rearrange("p (k s) -> p k s", k=4)).then_inc(gh_done, 1)

            def output_split(count):
                act.wait_ge(piece_used, count)
                for m in range(2):
                    nc.scalar.copy(ys_hi[:, 512 * m:512 * m + 512], bank[4 + m][:, :]).then_inc(ey_h, 1)

            gather_copies(1)
            act.wait_ge(routed, 1)
            n_items = act.value_load(items[0:1, 0:1], min_val=NE, max_val=MAX_ITEMS)
            q0 = MOE_BASE
            assert cur[0] == q0 + H
            act.wait_ge(cleared, 1)
            with act.Fori(0, n_items) as i:
                def item_split(lo, hi, r=None):
                    for n in range(lo, hi):
                        q = q0 + n
                        turn = 16 * (ITEM_CHUNKS // R) * i + 16 * (q // 2 // R + 1)
                        used = ITEM_PIECES * i + q - H + 1
                        if r is not None:
                            turn, used = turn + 16 * r, used + 12 * r
                        split(q, turn=turn, used=used)

                with act.If(i > 0):
                    item_split(0, H)
                output_split(ITEM_PIECES * i + q0)
                item_split(4, 8)
                act.wait_ge(piece_used, ITEM_PIECES * i + q0 + 4)
                nc.scalar.activation(sg[:, :], bank[0][:, :], ACT.Silu).then_inc(esg_done, 1)
                item_split(8, 12)
                act.wait_ge(pt_full, i + 1)
                nc.scalar.copy(perm_t, bank[7][:, 0:SEQ]).then_inc(pt_done, 1)
                with act.Fori(0, ESTEPS - 1) as r:
                    item_split(12, 14, r)
                    act.wait_ge(t_full, ESTEPS * i + r + 1)
                    nc.scalar.copy(eh_hi[:, :, :], bank[6][:, :].rearrange("p (k s) -> p k s", k=4)).then_inc(eh_h, 1)
                    item_split(14, 16, r)
                    act.wait_ge(piece_used, ITEM_PIECES * i + 12 * r + q0 + 12)
                    nc.scalar.activation(sg[:, :], bank[0][:, :], ACT.Silu).then_inc(esg_done, 1)
                    item_split(16, 24, r)
                act.wait_ge(t_full, ESTEPS * i + ESTEPS)
                nc.scalar.copy(eh_hi[:, :, :], bank[6][:, :].rearrange("p (k s) -> p k s", k=4)).then_inc(eh_h, 1)
                gather_copies(4 * i + 5)
            output_split(ITEM_PIECES * n_items + q0)
            norm_squares(4)

        @block.vector
        def _(dve):
            cur = [0]
            chain = [0]

            def step(ins):
                chain[0] += 1
                ins.then_inc(dve_step, 1)
                dve.wait_ge(dve_step, chain[0])

            def split(q, done=None):
                dve.wait_ge(hi_done, q + 1 if done is None else done)
                src = raw[:, q // 2 % R, (q % 2) * PIECE:(q % 2 + 1) * PIECE]
                nc.vector.tensor_tensor(w_lo[:, q % H, :], src, w_hi[:, q % H, :].bitcast(F32),
                                        ALU.subtract).then_inc(lo_done, 1)

            def until(q):
                while cur[0] < q:
                    n = cur[0]
                    split(n)
                    cur[0] += 1

            def full(l, name):
                if name in TURNED:
                    dve.wait_ge(turned, len(TURNED) * l + TURNED[name])
                else:
                    dve.wait_ge(piece_used, MIX_BASE[l] + UNIT_PIECES[name])
                return bank[(NU * l + UNIT[name]) % 4]

            def norm(n):
                for t in range(TB):
                    dve.wait_ge(sq_done, 2 * n + t + 1)
                    nc.vector.tensor_scalar(ss[:, t:t + 1], ss[:, t:t + 1], 1.0 / D, EPS, ALU.mult, ALU.add
                                            ).then_inc(ms_done, 1)
                    dve.wait_ge(rs_done, 2 * n + t + 1)
                    if t == 0:
                        dve.wait_ge(gain_in[n % 2], 16 * (n // 2 + 1))
                    nc.vector.scalar_tensor_tensor(out=hn[:, t, :], in0=x[:, t, :], scalar=rs[:, t:t + 1],
                                                   in1=gain[:, n % 2, :], op0=ALU.mult, op1=ALU.mult
                                                   ).then_inc(hn_done, 1)

            def norm_transposed(n):
                l, name = divmod(n, 2)
                for m in range(4):
                    src = bank[(NU * l + UNIT[f"n{name + 1}{m}"]) % 4]
                    dve.wait_ge(th_done, 4 * n + m + 1)
                    nc.vector.tensor_tensor(xt_lo[:, 2 * m:2 * m + 2, :], src[:, :].rearrange("p (k t) -> p k t", k=2),
                                            xt_hi[:, 2 * m:2 * m + 2, :].bitcast(F32), ALU.subtract
                                            ).then_inc(tl_done, 1)

            nc.vector.memset(zeros[:, :].bitcast(F32), 0.0).then_inc(init_done, 1)
            for l in range(DEPTH):
                base = MIX_BASE[l]
                taps = small[:, l, 0:CB * TAPS].rearrange("p (b j) -> p b j", b=CB)
                bias = small[:, l, CB * TAPS:CB * TAPS + HP]

                def after(chunk, base=base):
                    until(base + 2 * chunk + 2 + H)

                until(base + H)
                norm(2 * l)
                norm_transposed(2 * l)
                after(0)
                src = full(l, "alow")
                nc.vector.tensor_copy(al[0:RANK, :], src[0:RANK, 0:SEQ]).then_inc(al_done, 1)
                after(1)
                dve.wait_ge(z_full, l + 1)
                if l == 0:
                    dve.wait_ge(params_in, 80)
                for h in range(HP):
                    ins = nc.vector.tensor_scalar(zz[:, h, :], bank[4][:, h * SEQ:(h + 1) * SEQ], bias[:, h:h + 1],
                                                  None, ALU.add)
                ins.then_inc(z_read, 1)
                dve.wait_ge(z_read, l + 1)
                nc.vector.scalar_tensor_tensor(out=la[:, :, :], in0=zz[:, :, :], scalar=-1.0, in1=zz[:, :, :],
                                               op0=ALU.mult, op1=ALU.max).then_inc(abs_done, 1)
                after(2)
                dve.wait_ge(log_done, l + 1)
                step(nc.vector.scalar_tensor_tensor(out=zz[:, :, :], in0=zz[:, :, :], scalar=0.0, in1=la[:, :, :],
                                                    op0=ALU.min, op1=ALU.subtract))
                for h in range(HP):
                    ins = nc.vector.tensor_tensor_scan(bb[:, h, :], const[:, K_RESET:K_RESET + SEQ], zz[:, h, :],
                                                       0.0, ALU.mult, ALU.add)
                ins.then_inc(b_done, 1)
                after(6)
                step(nc.vector.memset(u[:, :, 0:2], 0.0))
                for n in range(2):
                    after(7 + n)
                    src = full(l, f"gc{n}")
                    dve.wait_ge(xc_done, 2 * l + n + 1)
                    nc.vector.tensor_tensor(u[:, 2 * n:2 * n + 2, 2:SEQ + 2], src[:, :].rearrange("p (b t) -> p b t", b=2),
                                            cv[:, 2 * n:2 * n + 2, :], ALU.mult).then_inc(gc_done, 1)
                    dve.wait_ge(gc_done, 2 * l + n + 1)
                for j in range(TAPS):
                    for b in range(CB):
                        if j == 0:
                            ins = nc.vector.tensor_scalar(cv[:, b, :], u[:, b, 0:SEQ], taps[:, b, 0:1], None, ALU.mult)
                        else:
                            ins = nc.vector.scalar_tensor_tensor(out=cv[:, b, :], in0=u[:, b, j:j + SEQ],
                                                                 scalar=taps[:, b, j:j + 1], in1=cv[:, b, :],
                                                                 op0=ALU.mult, op1=ALU.add)
                    step(ins)
                def scores(batch):
                    h, first = batch // 2, 4 * (batch % 2)
                    if batch == 0:
                        step(nc.vector.memset(sc[:, :, :, :], 0.0))
                    dve.wait_ge(sc_full, 4 * l + batch + 1)
                    for m in range(first, min(first + 4, NL + 1)):
                        mask = const[:, K_LVL + m * L:K_LVL + (m + 1) * L].bitcast(I32).unsqueeze(1)
                        for a in range(2):
                            at = (m - first) * TB * L
                            ins = nc.vector.copy_predicated(
                                sc[:, :, 2 * h + a, :], mask.to_broadcast([P, TB, L]),
                                bank[4 + a][:, at:at + TB * L].rearrange("p (t i) -> p t i", t=TB))
                        step(ins)
                    dve.sem_inc(sc_done, 1)

                for n in range(2):
                    after(9 + n)
                    src = full(l, f"gb{n}")
                    nc.vector.tensor_tensor(cv[:, 2 * n:2 * n + 2, :], src[:, :].rearrange("p (b t) -> p b t", b=2),
                                            cv[:, 2 * n:2 * n + 2, :], ALU.mult).then_inc(ya_made, 1)
                after(11)
                dve.wait_ge(ya_h, l + 1)
                nc.vector.tensor_tensor(ya_lo[:, :, :], cv[:, :, :], ya_hi[:, :, :].bitcast(F32), ALU.subtract
                                        ).then_inc(ya_l, 1)
                dve.wait_ge(ya_l, l + 1)
                for chunk in (12, 14):
                    after(chunk)
                    scores(chunk // 2 - 6)
                for h in range(HP):
                    dve.wait_ge(inc_full, l + 1)
                    if h == 0:
                        dve.wait_ge(eb_done, l + 1)
                    step(nc.vector.tensor_copy(st[:, 0, h, :], bank[6][:, h * DV:(h + 1) * DV]))
                    for c in range(1, NCH - 1):
                        last = c * L + L - 1
                        step(nc.vector.scalar_tensor_tensor(out=st[:, c, h, :], in0=st[:, c - 1, h, :],
                                                            scalar=eb[:, h, last:last + 1],
                                                            in1=bank[6 + c % 2][:, (c // 2 * 2 + h) * DV:(c // 2 * 2 + h + 1) * DV],
                                                            op0=ALU.mult, op1=ALU.add))
                dve.sem_inc(st_done, 1)
                for chunk in (17, 19):
                    after(chunk)
                    scores(chunk // 2 - 6)
                after(20)
                for t in range(TB):
                    dve.wait_ge(o_sq, TB * l + t + 1)
                    nc.vector.tensor_scalar(oss[:, t, :], oss[:, t, :], 1.0 / DV, EPS, ALU.mult, ALU.add
                                            ).then_inc(oms_done, 1)
                    dve.wait_ge(ors_done, TB * l + t + 1)
                    if t == 0:
                        dve.wait_ge(gs_done, l + 1)
                    for h in range(HEADS):
                        cols = slice(h * DV, (h + 1) * DV)
                        ins = nc.vector.scalar_tensor_tensor(out=yb[:, t, cols], in0=bank[6 + t][:, cols],
                                                             scalar=ors[:, t, h:h + 1], in1=gs[:, t, cols],
                                                             op0=ALU.mult, op1=ALU.mult)
                    ins.then_inc(yb_done, 1)

                def branch_a(n):
                    for m in range(2):
                        name = f"ya{2 * n + m}"
                        src = full(l, name)
                        kk = 4 * n + 2 * m
                        dve.wait_ge(gate_done, 8 * l + 2 * n + m + 1)
                        nc.vector.tensor_tensor(gate[:, 0, kk:kk + 2, :], gate[:, 0, kk:kk + 2, :],
                                                src[:, :].rearrange("p (b t) -> p b t", b=2), ALU.mult).then_inc(pa_done, 1)

                after(21)
                branch_a(0)
                for n in range(2):
                    dve.wait_ge(yt_h, 2 * l + n + 1)
                    src = full(l, f"yt{n}")
                    nc.vector.tensor_tensor(yb_lo[:, 2 * n:2 * n + 2, :], src[:, :].rearrange("p (b t) -> p b t", b=2),
                                            yb_hi[:, 2 * n:2 * n + 2, :].bitcast(F32), ALU.subtract).then_inc(yt_l, 1)
                after(22)
                branch_a(1)
                for n in range(2):
                    after(23 + n)
                    for m in range(2):
                        name = f"yb{2 * n + m}"
                        src = full(l, name)
                        kk = 4 * n + 2 * m
                        dve.wait_ge(gate_done, 8 * l + 4 + 2 * n + m + 1)
                        nc.vector.tensor_tensor(gate[:, 1, kk:kk + 2, :], gate[:, 1, kk:kk + 2, :],
                                                src[:, :].rearrange("p (b t) -> p b t", b=2), ALU.mult).then_inc(pb_done, 1)
                        dve.wait_ge(pb_done, 4 * l + 2 * n + m + 1)
                        if m == 0 and n == 0:
                            dve.wait_ge(pa_done, 4 * l + 4)
                        nc.vector.tensor_tensor(gate[:, 1, kk:kk + 2, :], gate[:, 1, kk:kk + 2, :],
                                                gate[:, 0, kk:kk + 2, :], ALU.add).then_inc(mg_made, 1)
                    for m in range(2):
                        kk = 4 * n + 2 * m
                        dve.wait_ge(mg_h, 4 * l + 2 * n + m + 1)
                        nc.vector.tensor_tensor(xt_lo[:, kk:kk + 2, :], gate[:, 1, kk:kk + 2, :],
                                                xt_hi[:, kk:kk + 2, :].bitcast(F32), ALU.subtract).then_inc(mg_l, 1)
                until(base + MIX_PIECES + H)
                for n in (0, 2, 1, 3):
                    t, half = n % 2, n // 2
                    name = f"wo{n}"
                    src = full(l, name)
                    cols = slice(512 * half, 512 * half + 512)
                    nc.vector.tensor_tensor(x[:, t, cols], x[:, t, cols], src[:, :], ALU.add).then_inc(x_new, 1)
                norm(2 * l + 1)
                norm_transposed(2 * l + 1)

                if l == 0:
                    def hidden(count, s, used):
                        dve.wait_ge(sg_done, count)
                        dve.wait_ge(piece_used, used)
                        nc.vector.tensor_tensor(hf[:, s, :], sg[:, :], bank[1][:, :], ALU.mult).then_inc(hf_done, 1)
                        dve.wait_ge(fh_h, count)
                        nc.vector.tensor_tensor(fh_lo[:, s, :, :], hf[:, s, :].rearrange("p (k t) -> p k t", k=2),
                                                fh_hi[:, s, :, :].bitcast(F32), ALU.subtract).then_inc(fh_l, 1)

                    q0 = FFN_BASE
                    until(q0 + 4 + H)
                    hidden(1, 0, q0 + 4)
                    with dve.Fori(0, (STEPS - 1) // 2) as r:
                        for s in range(2):
                            q = q0 + 4 + 6 * s + H
                            for n in range(4):
                                split(q + n, done=12 * r + q + n + 1)
                            hidden(2 * r + s + 2, 1 - s, 12 * r + q0 + 8 + 6 * s)
                            for n in range(4, 6):
                                split(q + n, done=12 * r + q + n + 1)
                    cur[0] = q0 + 4 + 6 * (STEPS - 1) + H
                    until(q0 + FFN_PIECES + H)
                    for n in range(4):
                        t, half = n // 2, n % 2
                        dve.wait_ge(piece_used, q0 + FFN_PIECES)
                        cols = slice(512 * half, 512 * half + 512)
                        nc.vector.tensor_tensor(x[:, t, cols], x[:, t, cols], bank[4 + n][:, :], ALU.add).then_inc(x_new, 1)

            dve.wait_ge(wr_h, 1)
            nc.vector.tensor_tensor(wr_lo[:, :, :], wr_raw[:, :, :], wr_hi[:, :, :].bitcast(F32), ALU.subtract
                                    ).then_inc(wr_l, 1)
            dve.wait_ge(hn_h, 1)
            nc.vector.tensor_tensor(hn_lo[:, :, :], hn[:, :, :], hn_hi[:, :, :].bitcast(F32), ALU.subtract
                                    ).then_inc(hn_l, 1)
            nc.vector.memset(keys[:, :, :], 0.0)
            nc.vector.memset(gates[:, :, :], 0.0)
            step(nc.vector.memset(perm_t.bitcast(F32), 0.0))

            def r2(at):
                return rt[:, at:at + TB]

            def r8(at):
                return rt[:, at:at + TB * NE].rearrange("p (b e) -> p b e", b=TB)

            lg, one1, one2, tmp = r8(0), r8(16), r8(32), r8(48)
            m1, m2, k1, pex, dif, p1, p2 = r2(68), r2(70), r2(72), r2(64), r2(66), r2(74), r2(76)
            mask, over, run, sel, cnt = r8(80), rt[:, 96:104], rt[:, 104:112], rt[:, 112:120], rt[:, 120:128]
            prod, fitems = r8(128), rt[:, 144:144 + 1 + MAX_ITEMS]
            rev = const[:, K_REV:K_REV + NE]
            dve.wait_ge(lg_full, 1)
            step(nc.vector.tensor_copy(lg, bank[4][:, 0:TB * NE].rearrange("p (b e) -> p b e", b=TB)))

            def pick(logits, best, one):
                step(nc.vector.tensor_reduce(best, logits, AX.X, ALU.max))
                for t in range(TB):
                    ins = nc.vector.scalar_tensor_tensor(out=tmp[:, t, :], in0=logits[:, t, :], scalar=best[:, t:t + 1],
                                                         in1=rev, op0=ALU.is_equal, op1=ALU.mult)
                step(ins)
                step(nc.vector.tensor_reduce(k1, tmp, AX.X, ALU.max))
                for t in range(TB):
                    ins = nc.vector.tensor_scalar(one[:, t, :], rev, k1[:, t:t + 1], None, ALU.is_equal)
                step(ins)

            pick(lg, m1, one1)
            step(nc.vector.scalar_tensor_tensor(out=lg, in0=one1, scalar=-3.0e38, in1=lg, op0=ALU.mult, op1=ALU.add))
            pick(lg, m2, one2)
            nc.vector.tensor_tensor(dif, m2, m1, ALU.subtract).then_inc(dif_done, 1)
            nc.vector.tensor_tensor(mask, one1, one2, ALU.add).then_inc(mask_done, 1)
            dve.wait_ge(pex_done, 1)
            step(nc.vector.tensor_scalar(p1, pex, 1.0, None, ALU.add))
            step(nc.vector.reciprocal(p1, p1))
            step(nc.vector.tensor_tensor(p2, pex, p1, ALU.mult))
            for t in range(TB):
                ins = nc.vector.tensor_scalar(gates[:, t, 1:1 + NE], one1[:, t, :], p1[:, t:t + 1], None, ALU.mult)
            step(ins)
            for t in range(TB):
                ins = nc.vector.scalar_tensor_tensor(out=gates[:, t, 1:1 + NE], in0=one2[:, t, :], scalar=p2[:, t:t + 1],
                                                     in1=gates[:, t, 1:1 + NE], op0=ALU.mult, op1=ALU.add)
            step(ins)
            dve.wait_ge(rank_full, 1)
            step(nc.vector.tensor_copy(cnt, bank[5][:, TB * NE:TB * NE + NE]))
            step(nc.vector.scalar_tensor_tensor(out=keys[:, :, 0:NE],
                                                in0=bank[5][:, 0:TB * NE].rearrange("p (b e) -> p b e", b=TB),
                                                scalar=1.0, in1=mask, op0=ALU.add, op1=ALU.mult))
            step(nc.vector.tensor_scalar(over, cnt, float(SLOTS), None, ALU.is_gt))
            step(nc.vector.tensor_tensor_scan(run, const[:, K_ONE:K_ONE + NE], over, 0.0, ALU.mult, ALU.add))
            nc.vector.tensor_copy(fitems[:, 1:1 + NE], const[:, K_EID:K_EID + NE])
            step(nc.vector.tensor_scalar(fitems[:, 0:1], run[:, NE - 1:NE], float(NE), None, ALU.add))
            for n in range(EXTRA):
                step(nc.vector.scalar_tensor_tensor(out=sel, in0=run, scalar=float(n + 1), in1=over,
                                                    op0=ALU.is_equal, op1=ALU.mult))
                for src, dst, off in ((keys[:, :, 0:NE], keys[:, :, NE + n:NE + n + 1], -float(SLOTS)),
                                      (gates[:, :, 1:1 + NE], gates[:, :, 1 + NE + n:2 + NE + n], 0.0)):
                    if dst.shape[2] == 0:
                        continue
                    for t in range(TB):
                        ins = nc.vector.tensor_tensor(prod[:, t, :], src[:, t, :], sel, ALU.mult)
                    step(ins)
                    for t in range(TB):
                        ins = nc.vector.tensor_reduce(dst[:, t, :], prod[:, t, :], AX.X, ALU.add)
                    step(ins)
                    step(nc.vector.tensor_scalar(dst, dst, off, None, ALU.add))
                step(nc.vector.tensor_tensor(prod[:, 0, :], sel, const[:, K_EID:K_EID + NE], ALU.mult))
                step(nc.vector.tensor_reduce(fitems[:, 1 + NE + n:2 + NE + n], prod[:, 0, :], AX.X, ALU.add))
            nc.vector.tensor_copy(items[:, :], fitems).then_inc(routed, 1)

            def make_perm(i):
                for t in range(TB):
                    ins = nc.vector.tensor_scalar(perm[:, t, :], const[:, K_IOTA:K_IOTA + SLOTS],
                                                  keys[:, t, i], None, ALU.is_equal)
                ins.then_inc(perm_done, 1)

            def gather_copies(count):
                for m in range(2):
                    dve.wait_ge(gather_full, count + m)
                    nc.vector.tensor_copy(ex_lo[:, 4 * m:4 * m + 4, :],
                                          bank[6 + m][:, :].rearrange("p (k s) -> p k s", k=4)).then_inc(gl_done, 1)

            def output_split(count):
                for m in range(2):
                    dve.wait_ge(ey_h, count + m + 1)
                    nc.vector.tensor_tensor(ys_lo[:, 512 * m:512 * m + 512], bank[4 + m][:, :],
                                            ys_hi[:, 512 * m:512 * m + 512].bitcast(F32), ALU.subtract).then_inc(ey_l, 1)

            def residual(first, count, i):
                for n in (first, first + 1):
                    t, half = n // 2, n % 2
                    cols = slice(512 * half, 512 * half + 512)
                    dve.wait_ge(scat_full, count + n + 1)
                    nc.vector.scalar_tensor_tensor(out=x[:, t, cols], in0=bank[6 + n % 2][:, :], scalar=gates[:, t, i],
                                                   in1=x[:, t, cols], op0=ALU.mult, op1=ALU.add).then_inc(scat_done, 1)

            dve.wait_ge(dve_step, chain[0])
            make_perm(slice(0, 1))
            gather_copies(3)
            dve.wait_ge(routed, 1)
            n_items = dve.value_load(items[0:1, 0:1], min_val=NE, max_val=MAX_ITEMS)
            q0 = MOE_BASE
            with dve.Fori(0, n_items) as i:
                def item_split(lo, hi, r=None):
                    for n in range(lo, hi):
                        done = ITEM_PIECES * i + q0 + n + 1
                        if r is not None:
                            done = done + 12 * r
                        split(q0 + n, done=done)

                with dve.If(i > 0):
                    item_split(0, H)
                output_split(2 * i)
                item_split(4, 8)
                residual(0, 4 * i, bass.ds(i, 1))
                item_split(8, 10)
                residual(2, 4 * i, bass.ds(i, 1))
                item_split(10, 12)

                def hidden(count, used):
                    dve.wait_ge(esg_done, count)
                    dve.wait_ge(piece_used, used)
                    nc.vector.tensor_tensor(hf[:, 0, :], sg[:, :], bank[1][:, :], ALU.mult).then_inc(ehf_done, 1)

                def hidden_lo(count):
                    dve.wait_ge(eh_h, count)
                    nc.vector.tensor_tensor(eh_lo[:, :, :], bank[6][:, :].rearrange("p (k s) -> p k s", k=4),
                                            eh_hi[:, :, :].bitcast(F32), ALU.subtract).then_inc(eh_l, 1)

                hidden(ESTEPS * i + 1, ITEM_PIECES * i + q0 + 8)
                with dve.Fori(0, ESTEPS - 1) as r:
                    item_split(12, 14, r)
                    hidden_lo(ESTEPS * i + r + 1)
                    item_split(14, 20, r)
                    hidden(ESTEPS * i + r + 2, ITEM_PIECES * i + 12 * r + q0 + 16)
                    item_split(20, 24, r)
                make_perm(bass.ds(i + 1, 1))
                hidden_lo(ESTEPS * i + ESTEPS)
                gather_copies(4 * i + 7)
            output_split(2 * n_items)
            residual(0, 4 * n_items, bass.ds(n_items, 1))
            residual(2, 4 * n_items, bass.ds(n_items, 1))
            dve.wait_ge(scat_done, 4 * n_items + 4)
            dve.sem_inc(x_new, 4)
            norm(4)

        @block.gpsimd
        def _(pool):
            chain = [0]

            def step(ins):
                chain[0] += 1
                ins.then_inc(pool_step, 1)
                pool.wait_ge(pool_step, chain[0])

            def root(n):
                for t in range(TB):
                    pool.wait_ge(ms_done, 2 * n + t + 1)
                    nc.gpsimd.tensor_tensor(rs[:, t:t + 1], ss[:, t:t + 1], const[:, K_PW:K_PW + 1], ALU.pow
                                            ).then_inc(rs_done, 1)

            pool.wait_ge(params_in, 80)
            for l in range(DEPTH):
                root(2 * l)
                for h in range(HP):
                    pool.wait_ge(b_done, l + 1)
                    b_h = bb[:, h, :]
                    for n, m in enumerate(LEVELS):
                        blk = b_h.rearrange("p (a s m) -> p a s m", s=2, m=m)
                        dst = ex[:, n, :].rearrange("p (a s m) -> p a s m", s=2, m=m)
                        mid = blk[:, :, 0, m - 1:m].to_broadcast([P, SEQ // (2 * m), m])
                        nc.gpsimd.tensor_tensor(dst[:, :, 0, :], mid, blk[:, :, 0, :], ALU.subtract)
                        nc.gpsimd.tensor_tensor(dst[:, :, 1, :], blk[:, :, 1, :], mid, ALU.subtract)
                    blk = b_h.rearrange("p (c m) -> p c m", m=L)
                    nc.gpsimd.tensor_tensor(ex[:, NL, :].rearrange("p (c m) -> p c m", m=L),
                                            blk[:, :, L - 1:L].to_broadcast([P, NCH, L]), blk, ALU.subtract
                                            ).then_inc(expo_done, 1)
                    pool.wait_ge(exp_done, HP * l + h + 1)
                    if h == 0:
                        pool.wait_ge(q_done, l + 1)
                        pool.wait_ge(k_done, l + 1)
                        if l:
                            pool.wait_ge(o_full, TB * l)
                    nc.gpsimd.tensor_tensor(kdT[:, h, :], kT[:, h, :], ex[:, NL, :], ALU.mult).then_inc(kd_made, 1)
                    if h == 0:
                        pool.wait_ge(eb_done, l + 1)
                        nc.gpsimd.tensor_tensor(qiT[:, :, :], qT[:, :, :], eb[:, :, :], ALU.mult).then_inc(qi_done, 1)
                    if h:
                        pool.wait_ge(sc_full, 4 * l + 2)
                    for n in range(NL):
                        nc.gpsimd.tensor_tensor(qe[:, n, :], qT[:, h, :], ex[:, n, :], ALU.mult)
                        ins = nc.gpsimd.tensor_tensor(ke[:, n, :], kT[:, h, :], ex[:, n, :], ALU.mult)
                    ins.then_inc(qk_done, 1)
                    pool.wait_ge(qk_done, HP * l + h + 1)
                pool.wait_ge(silu_done, 2 * l + 2)
                for t in range(TB):
                    g4 = gs[:, t, :].rearrange("p (h n) -> p h n", h=HEADS)
                    ins = nc.gpsimd.tensor_tensor(g4, g4, glag[:, l, :].unsqueeze(1).to_broadcast([P, HEADS, DV]), ALU.mult)
                ins.then_inc(gs_done, 1)
                for t in range(TB):
                    pool.wait_ge(oms_done, TB * l + t + 1)
                    nc.gpsimd.tensor_tensor(ors[:, t, :], oss[:, t, :], const[:, K_PW:K_PW + HEADS], ALU.pow
                                            ).then_inc(ors_done, 1)
                root(2 * l + 1)
            root(2 * DEPTH)

        @block.tensor
        def _(pe):
            def mm(out, lhs, rhs, first=False, last=False):
                return nc.tensor.matmul(out, lhs, rhs, start=first, stop=last, skip_group_check=True)

            def mm3(out, sta, mov, first=False, last=False):
                mm(out, sta[0], mov[0], first)
                mm(out, sta[0], mov[1])
                return mm(out, sta[1], mov[0], False, last)

            def piece(q, done=None):
                pe.wait_ge(lo_done, q + 1 if done is None else done)
                return w_hi[:, q % H, :], w_lo[:, q % H, :]

            def pair(p, f):
                return f(p[0]), f(p[1])

            nu = [0]

            def claim(l, name):
                n = NU * l + UNIT[name]
                assert n == nu[0], (n, nu[0], name)
                nu[0] += 1
                if n >= 4:
                    pe.wait_ge(*unit_read((n - 4) // NU, UNIT_NAMES[(n - 4) % NU]))
                return bank[n % 4]

            def norm_transposed(n):
                l, name = divmod(n, 2)
                for t in range(TB):
                    pe.wait_ge(hn_done, 2 * n + t + 1)
                for m in range(4):
                    out = claim(l, f"n{name + 1}{m}")
                    for k in range(2):
                        for t in range(TB):
                            kk = 2 * m + k
                            ins = nc.tensor.transpose(out[:, (2 * k + t) * P:(2 * k + t + 1) * P],
                                                      hn[:, t, kk * P:(kk + 1) * P], ident)
                    ins.then_inc(turned, 1)

            def channels(out, q0, blocks=2, counts=(None, None), ready=None):
                for half in range(2):
                    w = piece(q0 + half, counts[half])
                    w = pair(w, lambda a: a.rearrange("p (k n) -> p k n", k=4))
                    for k in range(4):
                        kk = 4 * half + k
                        if ready is not None and kk % 2 == 0:
                            pe.wait_ge(tl_done, ready + kk // 2 + 1)
                        for b in range(blocks):
                            ins = mm3(out[:, b * SEQ:(b + 1) * SEQ],
                                      pair(w, lambda a: a[:, k, b * P:(b + 1) * P]),
                                      (xt_hi[:, kk, :], xt_lo[:, kk, :]),
                                      kk == 0 and b == 0, kk == KT - 1 and b == blocks - 1)
                    ins.then_inc(piece_used, 1)

            def tokens(out, q0):
                for half in range(2):
                    w = pair(piece(q0 + half), lambda a: a.rearrange("p (k n) -> p k n", k=4))
                    for k in range(4):
                        kk = 4 * half + k
                        for t in range(TB):
                            ins = mm3(out[:, t * 256:(t + 1) * 256],
                                      (xt_hi[:, kk, t * P:(t + 1) * P], xt_lo[:, kk, t * P:(t + 1) * P]),
                                      pair(w, lambda a: a[:, k, :]), kk == 0 and t == 0, kk == KT - 1 and t == TB - 1)
                    ins.then_inc(piece_used, 1)

            pe.wait_ge(params_in, 80)
            pe.wait_ge(init_done, 1)
            for l in range(DEPTH):
                base = MIX_BASE[l]
                norm_transposed(2 * l)
                out = claim(l, "alow")
                channels(out, base, 1, ready=8 * l)

                def win(n, base=base, l=l):
                    name = WIN[n][0]
                    out = claim(l, name)
                    f = tokens if name[:2] in ("v0", "v1", "go") else channels
                    f(out, base + 2 + 2 * n)

                win(0)
                pe.wait_ge(al_done, l + 1)
                if l:
                    pe.wait_ge(sc_done, 4 * l)
                for h in range(HP):
                    ins = nc.tensor.matmul(bank[4][:, h * SEQ:(h + 1) * SEQ], wa2[:, l, h * P:(h + 1) * P],
                                           al[0:RANK, :], start=True, stop=True)
                ins.then_inc(z_full, 1)
                for n in range(1, 10):
                    win(n)
                def scores(batch):
                    h, first = batch // 2, 4 * (batch % 2)
                    if batch == 0:
                        pe.wait_ge(z_read, l + 1)
                    if 4 * l + batch:
                        pe.wait_ge(sc_done, 4 * l + batch)
                    pe.wait_ge(qk_done, HP * l + h + 1)
                    for m in range(first, min(first + 4, NL + 1)):
                        for c in range(NCH):
                            for a in range(2):
                                rows = slice(a * DK, (a + 1) * DK)
                                cols = slice(c * L, (c + 1) * L)
                                if m < NL:
                                    lhs, rhs = ke[rows, m, cols], qe[rows, m, cols]
                                else:
                                    lhs, rhs = kT[rows, h, cols], qT[rows, h, cols]
                                at = ((m - first) * TB + c // 2) * L
                                ins = nc.tensor.matmul(bank[4 + a][(c % 2) * L:(c % 2 + 1) * L, at:at + L], lhs, rhs,
                                                       start=True, stop=True)
                    ins.then_inc(sc_full, 1)

                win(10)
                for n in (11, 12, 13):
                    win(n)
                    if n != 12:
                        scores((n - 11) // 2)
                    if n == 12:
                        pe.wait_ge(kd_made, HP * l + HP)
                        pe.wait_ge(ya_l, l + 1)
                        if l:
                            pe.wait_ge(yb_done, TB * l)
                        for t in range(TB):
                            for h in range(HP):
                                at = (t * HP + h) * P
                                ins = nc.tensor.transpose(bank[7][:, at:at + P], kdT[:, h, t * P:(t + 1) * P], ident)
                        ins.then_inc(kdt_full, 1)
                pe.wait_ge(kdt_done, l + 1)
                pe.wait_ge(v_done, 2 * l + 2)
                for h in range(HP):
                    for c in range(NCH - 1):
                        for a in range(2):
                            rows = slice((c % 2) * L, (c % 2 + 1) * L)
                            head = 2 * h + a
                            at = (c // 2 * 2 + h) * DV
                            ins = nc.tensor.matmul(bank[6 + c % 2][a * DK:(a + 1) * DK, at:at + DV],
                                                   kd[rows, c // 2, h, a * DK:(a + 1) * DK],
                                                   v[rows, c // 2, head * DV:(head + 1) * DV], start=True, stop=True)
                ins.then_inc(inc_full, 1)
                win(14)
                for n in (15, 16, 17, 18):
                    win(n)
                    if n % 2 == 0:
                        scores(n // 2 - 6)
                win(19)
                pe.wait_ge(sc_done, 4 * (l + 1))
                pe.wait_ge(st_done, l + 1)
                pe.wait_ge(qi_done, l + 1)
                for t in range(TB):
                    for head in range(HEADS):
                        for c in range(2):
                            rows = slice(c * L, (c + 1) * L)
                            cols = slice(head * DV, (head + 1) * DV)
                            ins = mm(bank[6 + t][rows, cols], sc[rows, t, head, :], v[rows, t, cols], head == 0)
                ins.then_inc(o_part, 1)
                for a in range(2):
                    pe.wait_ge(o_part, 2 * l + a + 1)
                    krows = slice(a * DK, (a + 1) * DK)
                    for t in range(TB):
                        for h in range(HP):
                            for c in (2 * t, 2 * t + 1):
                                if c:
                                    head = 2 * h + a
                                    ins = mm(bank[6 + t][(c % 2) * L:(c % 2 + 1) * L, head * DV:(head + 1) * DV],
                                             qiT[krows, h, c * L:(c + 1) * L], st[krows, c - 1, h, :], False, a == 1)
                        if a == 1:
                            ins.then_inc(o_full, 1)
                    if a == 0:
                        ins.then_inc(o_part, 1)

                def branch(q0, y, first, names, l=l):
                    outs = [claim(l, name) for name in names]
                    for half in range(2):
                        w = pair(piece(q0 + half), lambda a: a.rearrange("p (k n) -> p k n", k=2))
                        for k in range(2):
                            kk = 2 * half + k
                            if first is not None and k == 0:
                                pe.wait_ge(yt_l, first + half + 1)
                            for b in range(4):
                                ins = mm3(outs[b // 2][:, b % 2 * SEQ:(b % 2 + 1) * SEQ],
                                          pair(w, lambda a: a[:, k, b * P:(b + 1) * P]),
                                          (y[0][:, kk, :], y[1][:, kk, :]), kk == 0 and b % 2 == 0,
                                          kk == CB - 1 and b % 2 == 1)
                        ins.then_inc(piece_used, 1)

                pe.wait_ge(ya_l, l + 1)
                q = base + 2 * (1 + len(WIN))
                branch(q, (ya_hi, ya_lo), None, ("ya0", "ya1"))

                def y_transposed(l=l):
                    for n in range(2):
                        out = claim(l, f"yt{n}")
                        for t in range(TB):
                            pe.wait_ge(yb_done, TB * l + t + 1)
                        for k in range(2):
                            for t in range(TB):
                                kk = 2 * n + k
                                ins = nc.tensor.transpose(out[:, (2 * k + t) * P:(2 * k + t + 1) * P],
                                                          yb[:, t, kk * P:(kk + 1) * P], ident)
                        ins.then_inc(turned, 1)

                y_transposed()
                branch(q + 2, (ya_hi, ya_lo), None, ("ya2", "ya3"))
                branch(q + 4, (yb_hi, yb_lo), 2 * l, ("yb0", "yb1"))
                branch(q + 6, (yb_hi, yb_lo), 2 * l, ("yb2", "yb3"))
                q += 8
                outs = [claim(l, f"wo{n}") for n in range(4)]
                for kh in range(2):
                    for half in range(2):
                        for s in range(2):
                            w = pair(piece(q), lambda a: a.rearrange("p (k n) -> p k n", k=2))
                            if half == 0:
                                pe.wait_ge(mg_l, 4 * l + 2 * kh + s + 1)
                            for t in range(TB):
                                for k in range(2):
                                    kk = 4 * kh + 2 * s + k
                                    ins = mm3(outs[2 * half + t][:, :],
                                              (xt_hi[:, kk, t * P:(t + 1) * P], xt_lo[:, kk, t * P:(t + 1) * P]),
                                              pair(w, lambda a: a[:, k, :]), kk == 0, kk == KT - 1)
                            ins.then_inc(piece_used, 1)
                            q += 1
                norm_transposed(2 * l + 1)

                if l == 0:
                    q0 = FFN_BASE
                    pe.wait_ge(tl_done, 8)
                    for n in range(4):
                        if n == 2:
                            pe.wait_ge(yb_done, TB * (l + 1))
                        mm(bank[4 + n][:, :], zeros[:, 0:P], zeros[:, :], True)

                    def up(q, counts, free, ready=None):
                        if free is not None:
                            pe.wait_ge(sg_done, free)
                        channels(bank[0], q, counts=counts[0:2], ready=ready)
                        if free is not None:
                            pe.wait_ge(hf_done, free)
                        channels(bank[1], q + 2, counts=counts[2:4])

                    def down(q, s, counts, count, last=False):
                        pe.wait_ge(fh_l, count)
                        for k in range(2):
                            w = piece(q + k, done=counts[k])
                            for t in range(TB):
                                for half in range(2):
                                    ins = mm3(bank[4 + 2 * t + half][:, :],
                                              (fh_hi[:, s, k, t * P:(t + 1) * P], fh_lo[:, s, k, t * P:(t + 1) * P]),
                                              pair(w, lambda a: a[:, 512 * half:512 * half + 512]), False, last)
                            ins.then_inc(piece_used, 1)

                    up(q0, (None,) * 4, None, ready=4)
                    with pe.Fori(0, (STEPS - 1) // 2) as r:
                        for s in range(2):
                            q = q0 + 4 + 6 * s
                            counts = [12 * r + q + n + 1 for n in range(6)]
                            up(q, counts, 2 * r + s + 1)
                            down(q + 4, s, counts[4:], 2 * r + s + 1)
                    down(q0 + FFN_PIECES - 2, 0, (None, None), STEPS, True)

            pe.wait_ge(wr_l, 1)
            pe.wait_ge(tl_done, 16)
            for t in range(TB):
                for k in range(KT):
                    ins = mm3(bank[4][:, t * NE:(t + 1) * NE],
                              (xt_hi[:, k, t * P:(t + 1) * P], xt_lo[:, k, t * P:(t + 1) * P]),
                              (wr_hi[:, k, :], wr_lo[:, k, :]), k == 0 and t == 0, k == KT - 1 and t == TB - 1)
            ins.then_inc(lg_full, 1)
            pe.wait_ge(mask_done, 1)
            masks = rt[:, 80:96].rearrange("p (b e) -> p b e", b=TB)
            tri = const[:, K_TRI:K_TRI + P]
            nc.tensor.matmul(bank[5][:, 0:NE], tri, masks[:, 0, :], start=True, stop=True)
            nc.tensor.matmul(bank[5][:, NE:2 * NE], tri, masks[:, 1, :], start=True, stop=False)
            nc.tensor.matmul(bank[5][:, NE:2 * NE], ones, masks[:, 0, :], start=False, stop=True)
            nc.tensor.matmul(bank[5][:, 2 * NE:3 * NE], ones, masks[:, 0, :], start=True, stop=False)
            nc.tensor.matmul(bank[5][:, 2 * NE:3 * NE], ones, masks[:, 1, :], start=False, stop=True
                             ).then_inc(rank_full, 1)

            def gather(m, src, first=None):
                for d in range(4):
                    dd = 4 * (m % 2) + d
                    for t in range(TB):
                        ins = mm(bank[6 + m % 2][:, d * SLOTS:(d + 1) * SLOTS], src[:, t, dd * P:(dd + 1) * P],
                                 perm[:, t, :], d == 0 and t == 0, d == 3 and t == TB - 1)
                ins.then_inc(gather_full, 1)

            def clear_output():
                for m in range(2):
                    ins = mm(bank[4 + m][:, :], zeros[:, 0:P], zeros[:, :], True)
                return ins

            def scatter(first, i, lo_count):
                for n in (first, first + 1):
                    t, half = n // 2, n % 2
                    if n < 2:
                        pe.wait_ge(ey_l, lo_count + n + 1)
                    if n == 0:
                        pe.wait_ge(gl_done, 2 * i + 2)
                    if n >= 2:
                        pe.wait_ge(scat_done, 4 * i + n - 1)
                    cols = slice(512 * half, 512 * half + 512)
                    lhs = perm_t[:, t * P:(t + 1) * P]
                    mm(bank[6 + n % 2][:, :], lhs, ys_hi[:, cols], True)
                    mm(bank[6 + n % 2][:, :], lhs, ys_lo[:, cols], False, True).then_inc(scat_full, 1)

            pe.wait_ge(rank_full, 1)
            pe.wait_ge(routed, 1)
            clear_output().then_inc(cleared, 1)
            pe.wait_ge(perm_done, 1)
            pe.wait_ge(hn_l, 1)
            gather(0, hn_hi)
            gather(1, hn_hi)
            pe.wait_ge(gh_done, 1)
            gather(2, hn_lo)
            pe.wait_ge(gh_done, 2)
            gather(3, hn_lo)
            n_items = pe.value_load(items[0:1, 0:1], min_val=NE, max_val=MAX_ITEMS)
            q0 = MOE_BASE
            with pe.Fori(0, n_items) as i:
                def done(n, r=None):
                    d = ITEM_PIECES * i + q0 + n + 1
                    return d if r is None else d + 12 * r

                def expert_up(out, n0, halves, r=None):
                    for s in halves:
                        w = pair(piece(q0 + n0 + s, done=done(n0 + s, r)), lambda a: a.rearrange("p (k n) -> p k n", k=2))
                        for k in range(2):
                            kk = 2 * s + k
                            ins = mm3(out[:, :], (ex_hi[:, kk, :], ex_lo[:, kk, :]),
                                      pair(w, lambda a: a[:, k, :]), kk == 0, kk == KT - 1)
                        ins.then_inc(piece_used, 1)

                def transposes(count, free=None):
                    pe.wait_ge(ehf_done, count)
                    for k in range(4):
                        ins = nc.tensor.transpose(bank[6][:, k * P:(k + 1) * P], hf[:, 0, k * P:(k + 1) * P], ident)
                    ins.then_inc(t_full, 1)

                def expert_down(n0, count, halves, r=None):
                    for s in halves:
                        if s == 0:
                            pe.wait_ge(eh_l, count)
                        w = piece(q0 + n0 + s, done=done(n0 + s, r))
                        for half in range(2):
                            ins = mm3(bank[4 + half][:, :], (eh_hi[:, s, :], eh_lo[:, s, :]),
                                      pair(w, lambda a: a[:, 512 * half:512 * half + 512]), False, False)
                        ins.then_inc(piece_used, 1)

                pe.wait_ge(gl_done, 2 * i + 2)
                pe.wait_ge(gh_done, 2 * i + 2)
                expert_up(bank[0], 0, range(4))
                scatter(0, i, 2 * i)
                expert_up(bank[1], 4, range(2))
                scatter(2, i, 2 * i)
                expert_up(bank[1], 4, range(2, 4))
                pe.wait_ge(scat_done, 4 * i + 4)
                for t in range(TB):
                    ins = nc.tensor.transpose(bank[7][:, t * P:(t + 1) * P], perm[:, t, :].bitcast(F32), ident)
                ins.then_inc(pt_full, 1)
                clear_output()
                with pe.Fori(0, ESTEPS - 1) as r:
                    pe.wait_ge(esg_done, ESTEPS * i + r + 1)
                    expert_up(bank[0], 8, range(2), r)
                    transposes(ESTEPS * i + r + 1)
                    expert_up(bank[0], 8, range(2, 4), r)
                    expert_up(bank[1], 12, range(4), r)
                    expert_down(16, ESTEPS * i + r + 1, range(4), r)
                transposes(ESTEPS * i + ESTEPS)
                pe.wait_ge(perm_done, i + 2)
                pe.wait_ge(eh_l, ESTEPS * i + ESTEPS)
                pe.wait_ge(pt_done, i + 1)
                gather(0, hn_hi)
                gather(1, hn_hi)
                expert_down(80, ESTEPS * i + ESTEPS, range(2))
                pe.wait_ge(gh_done, 2 * i + 4)
                gather(2, hn_lo)
                gather(3, hn_lo)
                expert_down(80, ESTEPS * i + ESTEPS, range(2, 4))
            scatter(0, n_items, 2 * n_items)
            scatter(2, n_items, 2 * n_items)


def kernel(**inputs):
    import concourse.bacc as _bacc
    from concourse.bass_utils import run_bass_kernel_spmd as _run

    nc = _bacc.Bacc("TRN2", target_bir_lowering=False, num_devices=1, dynamic_dma_scratch_size=1024)
    a = {name: np.ascontiguousarray(value) for name, value in inputs.items()}
    taps = a["conv_w"].transpose(0, 2, 1).reshape(DEPTH, CB, P, TAPS).transpose(0, 2, 1, 3).reshape(DEPTH, P, CB * TAPS)
    bias = a["b_a"].reshape(DEPTH, HP, P).transpose(0, 2, 1)
    feed = [("x", a["x"]), ("ln1", a["ln1_g"]), ("w_in", a["w_in"]), ("w_a2", a["w_a2"]),
            ("small", np.ascontiguousarray(np.concatenate([taps, bias], axis=2))), ("gla_g", a["gla_norm_g"]),
            ("w_br", a["w_branch"]), ("w_out", a["w_out"]), ("ln2", a["ln2_g"]), ("fg", a["ffn_w_gate"]),
            ("fu", a["ffn_w_up"]), ("fd", a["ffn_w_down"]), ("w_r", a["w_router"]), ("eg", a["moe_w_gate"]),
            ("eu", a["moe_w_up"]), ("ed", a["moe_w_down"]), ("fin", a["final_g"]), ("const", constants())]
    arrays = {f"in_{name}_dram": value for name, value in feed}
    args = [nc.dram_tensor(name, value.shape, F32, kind="ExternalInput").ap() for name, value in arrays.items()]
    args.append(nc.dram_tensor("out_0_dram", (1, SEQ, D), F32, kind="ExternalOutput").ap())
    trunk(nc, *args)
    r = _run(nc, [arrays], core_ids=[0])
    return r.results[0]["out_0_dram"]
```

```python
from contextlib import ExitStack

import numpy as np

import concourse.bass as bass
from concourse import mybir

F32 = mybir.dt.float32
F32R = mybir.dt.float32r
I32 = mybir.dt.int32
ALU = mybir.AluOpType
ACT = mybir.ActivationFunctionType
AX = mybir.AxisListType

P = 128
D = 1024
SEQ = 256
TB = SEQ // P
KT = D // P
DEPTH = 2
CONV = 512
CB = CONV // P
TAPS = 3
HEADS = 4
DK = 64
DV = 128
KW = HEADS * DK
VW = HEADS * DV
HP = HEADS // 2
RANK = 16
TAU = 16.0
L = 64
NCH = SEQ // L
FF = 2816
NE = 8
TOPK = 2
FFE = 3584
EPS = 1e-6
LEVELS = [32, 16, 8, 4, 2, 1]
NL = len(LEVELS)

CHUNK = 2048
PIECE = CHUNK // 2
R = 6
R2 = 2 * R
H = 4

C_X, C_GB, C_GC = 0, CONV, 2 * CONV
C_Q = 3 * CONV
C_K = C_Q + KW
C_V = C_K + KW
C_GO = C_V + VW
C_AL = C_GO + VW
C_GA = C_AL + RANK
C_GBR = C_GA + D

WIN = ([("q", C_Q), ("k", C_K), ("v0", C_V), ("v1", C_V + 256), ("xc0", C_X), ("xc1", C_X + 256),
        ("gc0", C_GC), ("gc1", C_GC + 256), ("gb0", C_GB), ("gb1", C_GB + 256),
        ("go0", C_GO), ("go1", C_GO + 256)]
       + [(f"ga{n}", C_GA + 256 * n) for n in range(4)] + [(f"gr{n}", C_GBR + 256 * n) for n in range(4)])
MIX_CHUNKS = 1 + len(WIN) + 4 + 4
MIX_PIECES = 2 * MIX_CHUNKS
UNIT_NAMES = (["alow"] + [w[0] for w in WIN] + [f"ya{n}" for n in range(4)] + [f"yb{n}" for n in range(4)]
              + [f"wo{n}" for n in range(4)])
UNIT = {name: n for n, name in enumerate(UNIT_NAMES)}
UNIT_PIECES = {"alow": 2, **{w[0]: 4 + 2 * n for n, w in enumerate(WIN)}, "ya0": 44, "ya1": 44, "ya2": 46, "ya3": 46,
               "yb0": 48, "yb1": 48, "yb2": 50, "yb3": 50, "wo0": 56, "wo1": 56, "wo2": 58, "wo3": 58}
N_TURNED = 10

STEPS = FF // 256
FFN_PIECES = 6 * STEPS
ESTEPS = FFE // 512
ITEM_CHUNKS = 6 * ESTEPS
ITEM_PIECES = 2 * ITEM_CHUNKS
SLOTS = 128
EXTRA = (SEQ * TOPK) // (SLOTS + 1)
MAX_ITEMS = NE + EXTRA

MIX_BASE = [0, MIX_PIECES + FFN_PIECES]
FFN_BASE = MIX_PIECES
MOE_BASE = 2 * MIX_PIECES + FFN_PIECES
assert H == 4 and R == 6 and (ITEM_CHUNKS % R, ITEM_PIECES % H, ITEM_CHUNKS // R % 2) == (0, 0, 1)

K_ID, K_PW = 0, 128
K_BASE = K_PW + HEADS
K_TRI, K_ONE, K_IOTA, K_RESET = (K_BASE + P * n for n in range(4))
K_LVL = K_RESET + SEQ
K_REV = K_LVL + (NL + 1) * L
K_EID = K_REV + NE
K_END = K_EID + NE


def constants():
    c = np.zeros((P, K_END), np.float32)
    a = np.arange(P)
    c[:, K_ID:K_ID + P] = a[:, None] == a[None, :]
    c[:, K_TRI:K_TRI + P] = a[:, None] < a[None, :]
    c[:, K_ONE:K_ONE + P] = 1.0
    c[:, K_IOTA:K_IOTA + P] = a[None, :] + 1
    c[:, K_RESET:K_RESET + SEQ] = (np.arange(SEQ) % L != 0)[None, :]
    j, i = (a % L)[:, None], np.arange(L)[None, :]
    for n, m in enumerate(LEVELS):
        c[:, K_LVL + n * L:K_LVL + (n + 1) * L] = (j // (2 * m) == i // (2 * m)) & (i // m % 2 == 1) & (j // m % 2 == 0)
    c[:, K_LVL + NL * L:K_LVL + (NL + 1) * L] = j == i
    c[:, K_REV:K_REV + NE] = NE - np.arange(NE)[None, :]
    c[:, K_EID:K_EID + NE] = np.arange(NE)[None, :]
    c[:, K_PW:K_PW + HEADS] = -0.5
    return c


def trunk(nc, x_d, ln1_d, w_in_d, w_a2_d, small_d, gla_g_d, w_br_d, w_out_d, ln2_d, fg_d, fu_d, fd_d,
          w_r_d, eg_d, eu_d, ed_d, fin_d, const_d, out_d):
    with ExitStack() as ctx:
        def sb(name, shape, dt=F32):
            return ctx.enter_context(nc.sbuf_tensor(name, shape, dt))

        def sem(name):
            return ctx.enter_context(nc.semaphore(name))

        bank = [ctx.enter_context(nc.psum_tensor(f"bank{n}", [P, 512], F32)) for n in range(8)]

        WORK = 17160
        mem = sb("mem", [P, R * CHUNK + WORK])

        def raw(slot, first=0, size=CHUNK):
            if isinstance(slot, int):
                return mem[:, slot * CHUNK + first:slot * CHUNK + first + size]
            return mem[:, bass.ds(slot * CHUNK + first, size)]
        w_hi = sb("w_hi", [P, H, PIECE], F32R)
        w_lo = sb("w_lo", [P, H, PIECE], F32R)
        const = sb("const", [P, K_END])
        x = sb("x", [P, TB, D])
        gain = sb("gain", [P, 2, D])
        xt_hi = sb("xt_hi", [P, KT, SEQ], F32R)
        xt_lo = sb("xt_lo", [P, KT, SEQ], F32R)
        area = sb("area", [P, 6144], F32R)
        ya_hi, ya_lo = (area[:, n * 1024:(n + 1) * 1024].rearrange("p (b t) -> p b t", b=CB) for n in (0, 1))
        yb_hi, yb_lo = (area[:, n * 1024:(n + 1) * 1024].rearrange("p (b t) -> p b t", b=CB) for n in (2, 3))
        fh_hi, fh_lo = (area[:, n * 1024:(n + 1) * 1024].rearrange("p (s k t) -> p s k t", s=2, k=2) for n in (0, 1))
        hn_hi, hn_lo = (area[:, n * 2048:(n + 1) * 2048].rearrange("p (b d) -> p b d", b=TB) for n in (0, 1))
        eh_hi, eh_lo = (area[:, 4096 + n * 512:4096 + (n + 1) * 512].rearrange("p (k s) -> p k s", k=4) for n in (0, 1))
        perm = area[:, 5120:5376].rearrange("p (b s) -> p b s", b=TB)
        perm_t = area[:, 5376:5632]
        ex_hi, ex_lo = (t[:, 0:4, :].rearrange("p k t -> p (k t)").rearrange("p (k s) -> p k s", k=KT)
                        for t in (xt_hi, xt_lo))
        ys_hi, ys_lo = (t[:, 4:8, :].rearrange("p k t -> p (k t)") for t in (xt_hi, xt_lo))
        zeros = sb("zeros", [P, 512], F32R)
        wr_hi = sb("wr_hi", [P, KT, NE], F32R)
        wr_lo = sb("wr_lo", [P, KT, NE], F32R)
        wr_raw = sb("wr_raw", [P, KT, NE])

        def carve(at, *shape):
            n = int(np.prod(shape))
            flat = mem[:, R * CHUNK + at:R * CHUNK + at + n]
            if len(shape) == 1:
                return flat
            names = "abcd"[:len(shape)]
            spec = f"p ({' '.join(names)}) -> p {' '.join(names)}"
            return flat.rearrange(spec, **dict(zip(names, shape)))

        qT, kT = carve(0, HP, SEQ), carve(512, HP, SEQ)
        v = carve(1024, TB, VW)
        gs = carve(2048, TB, VW)
        qe, ke = carve(3072, NL, SEQ), carve(4608, NL, SEQ)
        yb = carve(3072, TB, VW)
        ex = carve(6144, NL + 1, SEQ)
        kdT, qiT = carve(8192, HP, SEQ), carve(8704, HP, SEQ)
        u = carve(9216, CB, SEQ + 2)
        cv = carve(10248, CB, SEQ)
        kd = carve(9216, TB, HP, P)
        st = carve(9728, NCH - 1, HP, DV)
        sc = carve(10496, TB, HEADS, L)
        bb, zz, la = carve(11272, HP, SEQ), carve(11784, HP, SEQ), carve(12296, HP, SEQ)
        eb = la
        al = carve(12808, SEQ)
        KEPT = WORK - 4096
        assert KEPT >= max(R * CHUNK, 12808 + SEQ)
        hn = carve(KEPT, TB, D)
        gate = carve(KEPT, 2, KT, SEQ)
        sg = carve(KEPT + 2048, 512)
        hf = carve(KEPT + 2560, 2, 512)
        rt = carve(KEPT + 3584, 512)

        small = sb("small", [P, DEPTH, CB * TAPS + HP])
        wa2 = sb("wa2", [RANK, DEPTH, KW])
        glag = sb("glag", [P, DEPTH, DV])
        ss = sb("ss", [P, 2 * TB])
        ms = sb("ms", [P, TB])
        rs = sb("rs", [P, TB])
        oss = sb("oss", [P, TB, HEADS])
        ors = sb("ors", [P, TB, HEADS])
        keys = sb("keys", [P, TB, MAX_ITEMS + 1])
        gates = sb("gates", [P, TB, MAX_ITEMS + 1])
        items = sb("items", [P, 1 + MAX_ITEMS], I32)

        ident = const[:, K_ID:K_ID + P]
        ones = const[:, K_ONE:K_ONE + P]

        params_in = sem("params_in")
        base_in = sem("base_in")
        x_in = [sem("x_in0"), sem("x_in1")]
        gain_in = [sem("gain_in0"), sem("gain_in1")]
        raw_in = [sem(f"raw_in{n}") for n in range(R)]
        hi_done, lo_done, piece_used = sem("hi_done"), sem("lo_done"), sem("piece_used")
        turned = sem("turned")
        y_full = sem("y_full")
        x_new = sem("x_new")
        sq_done, hn_done = sem("sq_done"), sem("hn_done")
        sq_half, ms_done, rs_done, oms_done, ors_done = (
            sem(n) for n in ("sq_half", "ms_done", "rs_done", "oms_done", "ors_done"))
        th_done, tl_done = sem("th_done"), sem("tl_done")
        dve_step, act_step, pool_step = sem("dve_step"), sem("act_step"), sem("pool_step")
        al_done, z_full, z_read, abs_done, log_done, b_done = (sem(n) for n in (
            "al_done", "z_full", "z_read", "abs_done", "log_done", "b_done"))
        q_done, k_done, v_done, xc_done, silu_done, gate_done, gs_done = (sem(n) for n in (
            "q_done", "k_done", "v_done", "xc_done", "silu_done", "gate_done", "gs_done"))
        eb_done, expo_done, exp_done, qk_done, kd_made, qi_done = (sem(n) for n in (
            "eb_done", "expo_done", "exp_done", "qk_done", "kd_made", "qi_done"))
        kdt_full, kdt_done, inc_full, st_done, sc_full, sc_done, o_full, o_sq, yb_done = (sem(n) for n in (
            "kdt_full", "kdt_done", "inc_full", "st_done", "sc_full", "sc_done", "o_full", "o_sq", "yb_done"))
        o_part = sem("o_part")
        gc_done, pa_done, pb_done = sem("gc_done"), sem("pa_done"), sem("pb_done")
        ya_made, ya_h, ya_l, yt_h, yt_l, mg_made, mg_h, mg_l = (sem(n) for n in (
            "ya_made", "ya_h", "ya_l", "yt_h", "yt_l", "mg_made", "mg_h", "mg_l"))
        sg_done, hf_done, fh_h, fh_l = (sem(n) for n in ("sg_done", "hf_done", "fh_h", "fh_l"))
        wr_h, wr_l, hn_h, hn_l, lg_full, dif_done, pex_done, mask_done, rank_full, routed, init_done = (
            sem(n) for n in ("wr_h", "wr_l", "hn_h", "hn_l", "lg_full", "dif_done", "pex_done", "mask_done",
                             "rank_full", "routed", "init_done"))
        rank_read = sem("rank_read")
        perm_done, gather_full, gh_done, gl_done, pt_full, pt_done = (sem(n) for n in (
            "perm_done", "gather_full", "gh_done", "gl_done", "pt_full", "pt_done"))
        esg_done, ehf_done, t_full, eh_h, eh_l = (sem(n) for n in (
            "esg_done", "ehf_done", "t_full", "eh_h", "eh_l"))
        cleared, ey_h, ey_l, scat_full, scat_done = (sem(n) for n in (
            "cleared", "ey_h", "ey_l", "scat_full", "scat_done"))
        stored = sem("stored")

        def unit_read(l, name):
            kind, n = (name, 0) if name in ("alow", "q", "k") else (name[:2], int(name[2:] or 0) if name[:1] != "v" else 0)
            if name in ("alow", "q", "k"):
                return {"alow": al_done, "q": q_done, "k": k_done}[name], l + 1
            if name[0] == "v":
                return v_done, 2 * l + int(name[1]) + 1
            if kind in ("xc", "gc", "gb", "go"):
                return {"xc": xc_done, "gc": gc_done, "gb": ya_made, "go": silu_done}[kind], 2 * l + n + 1
            if kind in ("ga", "gr"):
                return gate_done, 8 * l + 4 * (kind == "gr") + n + 1
            return {"ya": pa_done, "yb": pb_done}[kind], 4 * l + n + 1

        NORM_TURNED = [N_TURNED * (n // 2) + 6 * (n % 2) for n in range(4)]

        GATHER = (7, 0, 1, 7)

        def slot_of(c):
            return c % R + (R if c >= MOE_BASE // 2 else 0)

        def ring_half(n, i, r=0):
            return (i + r + (n // R + 1)) % 2

        block = ctx.enter_context(nc.Block())

        @block.sync
        def _(sp):
            def load(c, src, wait=None):
                if wait is not None:
                    sp.wait_ge(lo_done, wait)
                elif c >= R:
                    sp.wait_ge(lo_done, 2 * (c - R) + 2)
                dst = raw(c % R).rearrange("p (k n) -> p k n", k=src.shape[1])
                sp.dma_start(dst, src).then_inc(raw_in[c % R], 16)

            def rows(w, k0, nk, c0, ncol):
                return w[k0 * P:(k0 + nk) * P, c0:c0 + ncol].rearrange("(k p) n -> p k n", p=P)

            def load_gain(n, src):
                if n >= 2:
                    sp.wait_ge(hn_done, 4 * (n - 1))
                sp.dma_start(gain[:, n % 2, :], src.partition_broadcast(P)).then_inc(gain_in[n % 2], 16)

            for t in range(TB):
                sp.dma_start(x[:, t, :], x_d[0, t * P:(t + 1) * P, :]).then_inc(x_in[t], 16)
            sp.dma_start(const[:, 0:K_BASE], const_d[:, 0:K_BASE]).then_inc(base_in, 16)
            load_gain(0, ln1_d[0])
            load(0, rows(w_in_d[0], 0, KT, C_AL, 256))
            sp.dma_start(const[:, K_BASE:K_END], const_d[:, K_BASE:K_END]).then_inc(params_in, 16)
            sp.dma_start(small[:, :, :], small_d.rearrange("l p n -> p l n")).then_inc(params_in, 16)
            sp.dma_start(wa2[:, :, :], w_a2_d.rearrange("l r n -> r l n")).then_inc(params_in, 16)
            sp.dma_start(glag[:, :, :], gla_g_d.partition_broadcast(P)).then_inc(params_in, 16)
            sp.dma_start(wr_raw[:, :, :], w_r_d[0].rearrange("(k p) e -> p k e", p=P)).then_inc(params_in, 16)

            for l in range(DEPTH):
                c = MIX_BASE[l] // 2
                if l:
                    load(c, rows(w_in_d[l], 0, KT, C_AL, 256))
                c += 1
                for n, (_, col) in enumerate(WIN):
                    load(c + n, rows(w_in_d[l], 0, KT, col, 256))
                    if n == 12:
                        load_gain(2 * l + 1, ln2_d[l])
                c += len(WIN)
                for br in range(2):
                    for n in range(2):
                        load(c + 2 * br + n, rows(w_br_d[l, br], 0, CB, 512 * n, 512))
                c += 4
                for kh in range(2):
                    for n in range(2):
                        load(c + 2 * kh + n, rows(w_out_d[l], 4 * kh, 4, 512 * n, 512))
                if l == 0:
                    c = FFN_BASE // 2
                    load(c, rows(fg_d[0], 0, KT, 0, 256))
                    load(c + 1, rows(fu_d[0], 0, KT, 0, 256))
                    load_gain(2, ln1_d[1])
                    with sp.Fori(0, (STEPS - 1) // 2) as r:
                        for s in range(2):
                            for n in range(3):
                                cc = c + 2 + 3 * s + n
                                w = (fg_d, fu_d, fd_d)[n][0]
                                if n < 2:
                                    w = w.rearrange("(k p) (m n) -> m p k n", p=P, n=256)[bass.ds(2 * r + (s + 1), 1)]
                                else:
                                    w = w.rearrange("(m k p) n -> m p k n", p=P, k=2)[bass.ds(2 * r + s, 1)]
                                load(cc, w.rearrange("m p k n -> (m p) k n"), wait=12 * r + 2 * (cc - R) + 2)
                    load(c + 3 * STEPS - 1, rows(fd_d[0], 2 * (STEPS - 1), 2, 0, D))

            load_gain(4, fin_d)

            c = MOE_BASE // 2

            def load_slot(n, i, src, r=0):
                count = ITEM_CHUNKS * i + 6 * r + c + n
                sp.wait_ge(lo_done, 2 * (count - R2) + 2)
                sp.wait_ge(raw_in[(c + n) % R], 16 * (ITEM_CHUNKS // R * i + r + (c + n) // R))
                slot = ring_half(n, i, r) * R + (c + n) % R
                sp.dma_start(raw(slot).rearrange("p (k n) -> p k n", k=src.shape[1]), src
                             ).then_inc(raw_in[(c + n) % R], 16)

            def load_item(e, i):
                def gate_up(w, half, col):
                    w = w[0].rearrange("e (k p) n -> e p k n", p=P)[bass.ds(e, 1), :, 4 * half:4 * half + 4, col]
                    return w.rearrange("m p k n -> (m p) k n")

                def down(first):
                    w = ed_d[0].rearrange("e (k p) n -> e p k n", p=P)[bass.ds(e, 1), :, first]
                    return w.rearrange("m p k n -> (m p) k n")

                for n in range(4):
                    load_slot(n, i, gate_up((eg_d, eu_d)[n // 2], n % 2, slice(0, 512)))
                with sp.Fori(0, ESTEPS - 1) as r:
                    for n in range(4):
                        load_slot(4 + n, i, gate_up((eg_d, eu_d)[n // 2], n % 2, bass.ds(512 * r + 512, 512)), r)
                    for n in range(2):
                        load_slot(8 + n, i, down(bass.ds(4 * r + 2 * n, 2)), r)
                for n in range(2):
                    load_slot(ITEM_CHUNKS - 2 + n, i, down(slice(4 * (ESTEPS - 1) + 2 * n, 4 * (ESTEPS - 1) + 2 * n + 2)))

            sp.wait_ge(turned, N_TURNED + 6)
            with sp.Fori(0, NE) as i:
                load_item(i, i)
            sp.wait_ge(routed, 1)
            n_items = sp.value_load(items[0:1, 0:1], min_val=NE, max_val=MAX_ITEMS)
            with sp.If(n_items > NE):
                with sp.Fori(NE, n_items) as i:
                    e = sp.value_load(items[0:1, bass.ds(i + 1, 1)], min_val=0, max_val=NE - 1)
                    load_item(e, i)

            for n in range(2 * TB):
                t, cols = n // 2, slice(512 * (n % 2), 512 * (n % 2) + 512)
                sp.wait_ge(hn_done, 4 * 4 + n + 1)
                sp.dma_start(out_d[0, t * P:(t + 1) * P, cols], hn[:, t, cols]).then_inc(stored, 16)
            sp.wait_ge(stored, 16 * 2 * TB)

        @block.scalar
        def _(act):
            cur = [0]
            chain = [0]

            def step(ins):
                chain[0] += 1
                ins.then_inc(act_step, 1)
                act.wait_ge(act_step, chain[0])

            def split(q, turn=None, used=None, slot=None):
                c = q // 2
                if q % 2 == 0:
                    act.wait_ge(raw_in[c % R], 16 * (c // R + 1) if turn is None else turn)
                if used is not None:
                    act.wait_ge(piece_used, used)
                elif q >= H:
                    act.wait_ge(piece_used, q - H + 1)
                src = raw(slot_of(c) if slot is None else slot, q % 2 * PIECE, PIECE)
                nc.scalar.copy(w_hi[:, q % H, :], src).then_inc(hi_done, 1)

            def until(q):
                while cur[0] < q:
                    n = cur[0]
                    split(n)
                    cur[0] += 1

            def full(l, name):
                act.wait_ge(piece_used, MIX_BASE[l] + UNIT_PIECES[name])
                return bank[UNIT[name] % 4]

            def norm_squares(n, parts, done=0):
                for p in parts:
                    if n == 0:
                        act.wait_ge(x_in[p // 2], 16)
                    elif n < 4:
                        act.wait_ge(x_new, 4 * (n - 1) + p + 1)
                    else:
                        act.wait_ge(scat_done, done + p + 1)
                    cols = slice(512 * (p % 2), 512 * (p % 2) + 512)
                    nc.scalar.activation(hn[:, p // 2, cols], x[:, p // 2, cols], ACT.Square,
                                         accum_out=ss[:, p:p + 1]).then_inc(sq_done, 1)

            def norm_transposed(n, parts):
                for m in parts:
                    act.wait_ge(turned, NORM_TURNED[n] + m + 1)
                    nc.scalar.copy(xt_hi[:, 2 * m:2 * m + 2, :],
                                   bank[4 * (n % 2) + m][:, :].rearrange("p (k t) -> p k t", k=2)).then_inc(th_done, 1)

            for l in range(DEPTH):
                base = MIX_BASE[l]

                def after(chunk, base=base):
                    until(base + 2 * chunk + 2 + H)

                if l == 0:
                    norm_squares(0, range(4))
                else:
                    norm_squares(2, range(4))
                norm_transposed(2 * l, range(4))
                until(base + H)
                after(1)
                src = full(l, "q")
                nc.scalar.mul(qT[:, :, :], src[:, :].rearrange("p (b t) -> p b t", b=HP), DK ** -0.5).then_inc(q_done, 1)
                after(2)
                src = full(l, "k")
                nc.scalar.copy(kT[:, :, :], src[:, :].rearrange("p (b t) -> p b t", b=HP)).then_inc(k_done, 1)
                act.wait_ge(abs_done, l + 1)
                step(nc.scalar.activation(la[:, :, :], la[:, :, :], ACT.Exp, scale=-1.0))
                nc.scalar.activation(la[:, :, :], la[:, :, :], ACT.Ln, bias=1.0).then_inc(log_done, 1)
                for n in range(2):
                    after(3 + n)
                    src = full(l, f"v{n}")
                    nc.scalar.copy(v[:, :, 256 * n:256 * n + 256],
                                   src[:, :].rearrange("p (b n) -> p b n", b=TB)).then_inc(v_done, 1)
                act.wait_ge(b_done, l + 1)
                nc.scalar.activation(eb[:, :, :], bb[:, :, :], ACT.Exp, scale=1.0 / TAU).then_inc(eb_done, 1)
                for n in range(2):
                    after(5 + n)
                    src = full(l, f"xc{n}")
                    nc.scalar.copy(cv[:, 2 * n:2 * n + 2, :],
                                   src[:, :].rearrange("p (b t) -> p b t", b=2)).then_inc(xc_done, 1)
                for h in range(HP):
                    after(7 + 3 * h)
                    act.wait_ge(expo_done, HP * l + h + 1)
                    nc.scalar.activation(ex[:, :, :], ex[:, :, :], ACT.Exp, scale=1.0 / TAU).then_inc(exp_done, 1)
                after(11)
                act.wait_ge(ya_made, 2 * l + 2)
                nc.scalar.copy(ya_hi[:, :, :], cv[:, :, :]).then_inc(ya_h, 1)
                for n in range(2):
                    after(11 + n)
                    src = full(l, f"go{n}")
                    nc.scalar.activation(gs[:, :, 256 * n:256 * n + 256],
                                         src[:, :].rearrange("p (b n) -> p b n", b=TB), ACT.Silu).then_inc(silu_done, 1)
                for n in range(8):
                    after(13 + n)
                    if n == 1:
                        act.wait_ge(kdt_full, l + 1)
                        nc.scalar.copy(kd[:, :, :, :], bank[7][:, :].rearrange("p (b h n) -> p b h n", b=TB, h=HP)
                                       ).then_inc(kdt_done, 1)
                    name = f"{('ga', 'gr')[n // 4]}{n % 4}"
                    src = full(l, name)
                    nc.scalar.activation(gate[:, n // 4, 2 * (n % 4):2 * (n % 4) + 2, :],
                                         src[:, :].rearrange("p (b t) -> p b t", b=2), ACT.Sigmoid).then_inc(gate_done, 1)
                for t in range(TB):
                    act.wait_ge(o_full, TB * l + t + 1)
                    for h in range(HEADS):
                        ins = nc.scalar.activation(yb[:, t, h * DV:(h + 1) * DV], bank[6 + t][:, h * DV:(h + 1) * DV],
                                                   ACT.Square, accum_out=oss[:, t, h:h + 1])
                    ins.then_inc(o_sq, 1)
                after(21)
                for n in range(2):
                    act.wait_ge(turned, N_TURNED * l + 4 + n + 1)
                    nc.scalar.copy(yb_hi[:, 2 * n:2 * n + 2, :],
                                   bank[4 + n][:, :].rearrange("p (b t) -> p b t", b=2)).then_inc(yt_h, 1)
                for n in range(2):
                    after(23 + n)
                    for m in range(2):
                        act.wait_ge(mg_made, 4 * l + 2 * n + m + 1)
                        kk = 4 * n + 2 * m
                        nc.scalar.copy(xt_hi[:, kk:kk + 2, :], gate[:, 1, kk:kk + 2, :]).then_inc(mg_h, 1)
                until(base + MIX_PIECES)
                norm_squares(2 * l + 1, (0, 1))
                until(base + MIX_PIECES + 2)
                norm_squares(2 * l + 1, (2, 3))
                norm_transposed(2 * l + 1, range(4))
                until(base + MIX_PIECES + H)

                if l == 0:
                    act.wait_ge(params_in, 80)
                    nc.scalar.copy(wr_hi[:, :, :], wr_raw[:, :, :]).then_inc(wr_h, 1)
                    q0 = FFN_BASE
                    until(q0 + 2 + H)
                    act.wait_ge(piece_used, q0 + 2)
                    nc.scalar.activation(sg[:, :], bank[0][:, :], ACT.Silu).then_inc(sg_done, 1)
                    until(q0 + 4 + H)
                    act.wait_ge(hf_done, 1)
                    nc.scalar.copy(fh_hi[:, 0, :, :], hf[:, 0, :].rearrange("p (k t) -> p k t", k=2)).then_inc(fh_h, 1)
                    with act.Fori(0, (STEPS - 1) // 2) as r:
                        for s in range(2):
                            first = q0 + 4 + 6 * s

                            def loop_split(lo, hi, first=first):
                                for n in range(lo, hi):
                                    q = first + H + n
                                    split(q, turn=16 * r + 16 * (q // 2 // R + 1), used=12 * r + q - H + 1)
                            loop_split(0, 2)
                            act.wait_ge(piece_used, 12 * r + first + 2)
                            nc.scalar.activation(sg[:, :], bank[0][:, :], ACT.Silu).then_inc(sg_done, 1)
                            loop_split(2, 4)
                            act.wait_ge(hf_done, 2 * r + s + 2)
                            nc.scalar.copy(fh_hi[:, 1 - s, :, :],
                                           hf[:, 1 - s, :].rearrange("p (k t) -> p k t", k=2)).then_inc(fh_h, 1)
                            loop_split(4, 6)
                    cur[0] = q0 + 4 + 6 * (STEPS - 1) + H
                    until(q0 + FFN_PIECES + 2)

            nc.scalar.copy(hn_hi[:, :, :], hn[:, :, :]).then_inc(hn_h, 1)
            act.wait_ge(dif_done, 1)
            nc.scalar.activation(rt[:, 64:66], rt[:, 66:68], ACT.Exp).then_inc(pex_done, 1)
            def gather_copies(count):
                for m in range(2):
                    act.wait_ge(gather_full, count + m)
                    nc.scalar.copy(ex_hi[:, 4 * m:4 * m + 4, :],
                                   bank[GATHER[m]][:, :].rearrange("p (k s) -> p k s", k=4)).then_inc(gh_done, 1)

            def output_split(count):
                act.wait_ge(piece_used, count)
                for m in range(2):
                    nc.scalar.copy(ys_hi[:, 512 * m:512 * m + 512], bank[4 + m][:, :]).then_inc(ey_h, 1)

            gather_copies(1)
            act.wait_ge(routed, 1)
            n_items = act.value_load(items[0:1, 0:1], min_val=NE, max_val=MAX_ITEMS)
            q0 = MOE_BASE
            assert cur[0] == q0 + H
            act.wait_ge(cleared, 1)
            with act.Fori(0, n_items) as i:
                def item_split(lo, hi, r=None):
                    for n in range(lo, hi):
                        q = q0 + n
                        turn = 16 * (ITEM_CHUNKS // R) * i + 16 * (q // 2 // R + 1)
                        used = ITEM_PIECES * i + q - H + 1
                        if r is not None:
                            turn, used = turn + 16 * r, used + 12 * r
                        half = ring_half(n // 2, i, 0 if r is None else r)
                        split(q, turn=turn, used=used, slot=half * R + q // 2 % R)

                with act.If(i > 0):
                    item_split(0, H)
                output_split(ITEM_PIECES * i + q0)
                item_split(4, 8)
                act.wait_ge(piece_used, ITEM_PIECES * i + q0 + 4)
                nc.scalar.activation(sg[:, :], bank[0][:, :], ACT.Silu).then_inc(esg_done, 1)
                item_split(8, 12)
                act.wait_ge(pt_full, i + 1)
                nc.scalar.copy(perm_t, bank[7][:, 0:SEQ]).then_inc(pt_done, 1)
                with act.Fori(0, ESTEPS - 1) as r:
                    item_split(12, 14, r)
                    act.wait_ge(t_full, ESTEPS * i + r + 1)
                    nc.scalar.copy(eh_hi[:, :, :], bank[6][:, :].rearrange("p (k s) -> p k s", k=4)).then_inc(eh_h, 1)
                    item_split(14, 16, r)
                    act.wait_ge(piece_used, ITEM_PIECES * i + 12 * r + q0 + 12)
                    nc.scalar.activation(sg[:, :], bank[0][:, :], ACT.Silu).then_inc(esg_done, 1)
                    item_split(16, 24, r)
                act.wait_ge(t_full, ESTEPS * i + ESTEPS)
                nc.scalar.copy(eh_hi[:, :, :], bank[6][:, :].rearrange("p (k s) -> p k s", k=4)).then_inc(eh_h, 1)
                gather_copies(4 * i + 5)
            output_split(ITEM_PIECES * n_items + q0)
            norm_squares(4, range(4), 4 * n_items)

        @block.vector
        def _(dve):
            cur = [0]
            chain = [0]

            def step(ins):
                chain[0] += 1
                ins.then_inc(dve_step, 1)
                dve.wait_ge(dve_step, chain[0])

            def split(q, done=None, slot=None):
                dve.wait_ge(hi_done, q + 1 if done is None else done)
                src = raw(slot_of(q // 2) if slot is None else slot, q % 2 * PIECE, PIECE)
                nc.vector.tensor_tensor(w_lo[:, q % H, :], src, w_hi[:, q % H, :].bitcast(F32),
                                        ALU.subtract).then_inc(lo_done, 1)

            def until(q):
                while cur[0] < q:
                    n = cur[0]
                    split(n)
                    cur[0] += 1

            def full(l, name):
                dve.wait_ge(piece_used, MIX_BASE[l] + UNIT_PIECES[name])
                return bank[UNIT[name] % 4]

            def norm(n, add, between=None):
                def mean_square(t):
                    dve.wait_ge(sq_done, 4 * n + 2 * t + 1)
                    nc.vector.tensor_scalar(ms[:, t:t + 1], ss[:, 2 * t:2 * t + 1], 1.0 / D, EPS, ALU.mult, ALU.add
                                            ).then_inc(sq_half, 1)
                    dve.wait_ge(sq_half, 2 * n + t + 1)
                    dve.wait_ge(sq_done, 4 * n + 2 * t + 2)
                    nc.vector.scalar_tensor_tensor(out=ms[:, t:t + 1], in0=ss[:, 2 * t + 1:2 * t + 2], scalar=1.0 / D,
                                                   in1=ms[:, t:t + 1], op0=ALU.mult, op1=ALU.add).then_inc(ms_done, 1)

                def scaled(p):
                    t, cols = p // 2, slice(512 * (p % 2), 512 * (p % 2) + 512)
                    if p % 2 == 0:
                        dve.wait_ge(rs_done, 2 * n + t + 1)
                    if p == 0:
                        dve.wait_ge(gain_in[n % 2], 16 * (n // 2 + 1))
                    nc.vector.scalar_tensor_tensor(out=hn[:, t, cols], in0=x[:, t, cols], scalar=rs[:, t:t + 1],
                                                   in1=gain[:, n % 2, cols], op0=ALU.mult, op1=ALU.mult
                                                   ).then_inc(hn_done, 1)

                add(0)
                add(1)
                mean_square(0)
                if between is not None:
                    between()
                add(2)
                add(3)
                scaled(0)
                mean_square(1)
                for p in range(1, 4):
                    scaled(p)

            def norm_transposed(n, parts):
                for m in parts:
                    dve.wait_ge(th_done, 4 * n + m + 1)
                    nc.vector.tensor_tensor(xt_lo[:, 2 * m:2 * m + 2, :],
                                            bank[4 * (n % 2) + m][:, :].rearrange("p (k t) -> p k t", k=2),
                                            xt_hi[:, 2 * m:2 * m + 2, :].bitcast(F32), ALU.subtract
                                            ).then_inc(tl_done, 1)

            def residual_add(p, src, n):
                t, cols = p // 2, slice(512 * (p % 2), 512 * (p % 2) + 512)
                nc.vector.tensor_tensor(x[:, t, cols], x[:, t, cols], src[:, :], ALU.add).then_inc(x_new, 1)

            nc.vector.memset(zeros[:, :].bitcast(F32), 0.0).then_inc(init_done, 1)
            for l in range(DEPTH):
                base = MIX_BASE[l]
                taps = small[:, l, 0:CB * TAPS].rearrange("p (b j) -> p b j", b=CB)
                bias = small[:, l, CB * TAPS:CB * TAPS + HP]

                def after(chunk, base=base):
                    until(base + 2 * chunk + 2 + H)

                if l == 0:
                    norm(0, lambda p: None)
                else:
                    def add_ffn(p):
                        if p < 3:
                            dve.wait_ge(y_full, 1 + (1, 1, 2)[p])
                        else:
                            dve.wait_ge(piece_used, FFN_BASE + FFN_PIECES)
                        residual_add(p, bank[4 + p], 2)

                    norm(2, add_ffn)
                norm_transposed(2 * l, range(4))
                until(base + H)
                after(0)
                src = full(l, "alow")
                nc.vector.tensor_copy(al[0:RANK, :], src[0:RANK, 0:SEQ]).then_inc(al_done, 1)
                after(1)
                dve.wait_ge(z_full, l + 1)
                if l == 0:
                    dve.wait_ge(params_in, 80)
                for h in range(HP):
                    ins = nc.vector.tensor_scalar(zz[:, h, :], bank[4][:, h * SEQ:(h + 1) * SEQ], bias[:, h:h + 1],
                                                  None, ALU.add)
                ins.then_inc(z_read, 1)
                dve.wait_ge(z_read, l + 1)
                nc.vector.scalar_tensor_tensor(out=la[:, :, :], in0=zz[:, :, :], scalar=-1.0, in1=zz[:, :, :],
                                               op0=ALU.mult, op1=ALU.max).then_inc(abs_done, 1)
                after(2)
                dve.wait_ge(log_done, l + 1)
                step(nc.vector.scalar_tensor_tensor(out=zz[:, :, :], in0=zz[:, :, :], scalar=0.0, in1=la[:, :, :],
                                                    op0=ALU.min, op1=ALU.subtract))
                for h in range(HP):
                    ins = nc.vector.tensor_tensor_scan(bb[:, h, :], const[:, K_RESET:K_RESET + SEQ], zz[:, h, :],
                                                       0.0, ALU.mult, ALU.add)
                ins.then_inc(b_done, 1)
                after(6)
                step(nc.vector.memset(u[:, :, 0:2], 0.0))
                for n in range(2):
                    after(7 + n)
                    src = full(l, f"gc{n}")
                    dve.wait_ge(xc_done, 2 * l + n + 1)
                    nc.vector.tensor_tensor(u[:, 2 * n:2 * n + 2, 2:SEQ + 2], src[:, :].rearrange("p (b t) -> p b t", b=2),
                                            cv[:, 2 * n:2 * n + 2, :], ALU.mult).then_inc(gc_done, 1)
                    dve.wait_ge(gc_done, 2 * l + n + 1)
                for j in range(TAPS):
                    for b in range(CB):
                        if j == 0:
                            ins = nc.vector.tensor_scalar(cv[:, b, :], u[:, b, 0:SEQ], taps[:, b, 0:1], None, ALU.mult)
                        else:
                            ins = nc.vector.scalar_tensor_tensor(out=cv[:, b, :], in0=u[:, b, j:j + SEQ],
                                                                 scalar=taps[:, b, j:j + 1], in1=cv[:, b, :],
                                                                 op0=ALU.mult, op1=ALU.add)
                    step(ins)
                def scores(batch):
                    h, first = batch // 2, 4 * (batch % 2)
                    if batch == 0:
                        step(nc.vector.memset(sc[:, :, :, :], 0.0))
                    dve.wait_ge(sc_full, 4 * l + batch + 1)
                    for m in range(first, min(first + 4, NL + 1)):
                        mask = const[:, K_LVL + m * L:K_LVL + (m + 1) * L].bitcast(I32).unsqueeze(1)
                        for a in range(2):
                            at = (m - first) * TB * L
                            ins = nc.vector.copy_predicated(
                                sc[:, :, 2 * h + a, :], mask.to_broadcast([P, TB, L]),
                                bank[4 + a][:, at:at + TB * L].rearrange("p (t i) -> p t i", t=TB))
                        step(ins)
                    dve.sem_inc(sc_done, 1)

                for n in range(2):
                    after(9 + n)
                    src = full(l, f"gb{n}")
                    nc.vector.tensor_tensor(cv[:, 2 * n:2 * n + 2, :], src[:, :].rearrange("p (b t) -> p b t", b=2),
                                            cv[:, 2 * n:2 * n + 2, :], ALU.mult).then_inc(ya_made, 1)
                after(11)
                dve.wait_ge(ya_h, l + 1)
                nc.vector.tensor_tensor(ya_lo[:, :, :], cv[:, :, :], ya_hi[:, :, :].bitcast(F32), ALU.subtract
                                        ).then_inc(ya_l, 1)
                dve.wait_ge(ya_l, l + 1)
                for chunk in (12, 14):
                    after(chunk)
                    scores(chunk // 2 - 6)
                for h in range(HP):
                    dve.wait_ge(inc_full, l + 1)
                    if h == 0:
                        dve.wait_ge(eb_done, l + 1)
                    step(nc.vector.tensor_copy(st[:, 0, h, :], bank[6][:, h * DV:(h + 1) * DV]))
                    for c in range(1, NCH - 1):
                        last = c * L + L - 1
                        step(nc.vector.scalar_tensor_tensor(out=st[:, c, h, :], in0=st[:, c - 1, h, :],
                                                            scalar=eb[:, h, last:last + 1],
                                                            in1=bank[6 + c % 2][:, (c // 2 * 2 + h) * DV:(c // 2 * 2 + h + 1) * DV],
                                                            op0=ALU.mult, op1=ALU.add))
                dve.sem_inc(st_done, 1)
                for chunk in (17, 19):
                    after(chunk)
                    scores(chunk // 2 - 6)
                after(20)
                for t in range(TB):
                    dve.wait_ge(o_sq, TB * l + t + 1)
                    nc.vector.tensor_scalar(oss[:, t, :], oss[:, t, :], 1.0 / DV, EPS, ALU.mult, ALU.add
                                            ).then_inc(oms_done, 1)
                    dve.wait_ge(ors_done, TB * l + t + 1)
                    if t == 0:
                        dve.wait_ge(gs_done, l + 1)
                    for h in range(HEADS):
                        cols = slice(h * DV, (h + 1) * DV)
                        ins = nc.vector.scalar_tensor_tensor(out=yb[:, t, cols], in0=bank[6 + t][:, cols],
                                                             scalar=ors[:, t, h:h + 1], in1=gs[:, t, cols],
                                                             op0=ALU.mult, op1=ALU.mult)
                    ins.then_inc(yb_done, 1)

                def branch_a(n):
                    for m in range(2):
                        name = f"ya{2 * n + m}"
                        src = full(l, name)
                        kk = 4 * n + 2 * m
                        dve.wait_ge(gate_done, 8 * l + 2 * n + m + 1)
                        nc.vector.tensor_tensor(gate[:, 0, kk:kk + 2, :], gate[:, 0, kk:kk + 2, :],
                                                src[:, :].rearrange("p (b t) -> p b t", b=2), ALU.mult).then_inc(pa_done, 1)

                after(21)
                branch_a(0)
                for n in range(2):
                    dve.wait_ge(yt_h, 2 * l + n + 1)
                    nc.vector.tensor_tensor(yb_lo[:, 2 * n:2 * n + 2, :],
                                            bank[4 + n][:, :].rearrange("p (b t) -> p b t", b=2),
                                            yb_hi[:, 2 * n:2 * n + 2, :].bitcast(F32), ALU.subtract).then_inc(yt_l, 1)
                after(22)
                branch_a(1)
                for n in range(2):
                    for m in range(2):
                        src = full(l, f"yb{2 * n + m}")
                        kk = 4 * n + 2 * m
                        dve.wait_ge(gate_done, 8 * l + 4 + 2 * n + m + 1)
                        nc.vector.tensor_tensor(gate[:, 1, kk:kk + 2, :], gate[:, 1, kk:kk + 2, :],
                                                src[:, :].rearrange("p (b t) -> p b t", b=2), ALU.mult).then_inc(pb_done, 1)
                    until(base + 2 * (23 + n) + 1 + H)
                    for m in range(2):
                        kk = 4 * n + 2 * m
                        dve.wait_ge(pb_done, 4 * l + 2 * n + m + 1)
                        if m == 0:
                            dve.wait_ge(pa_done, 4 * l + 2 * n + 2)
                        nc.vector.tensor_tensor(gate[:, 1, kk:kk + 2, :], gate[:, 1, kk:kk + 2, :],
                                                gate[:, 0, kk:kk + 2, :], ALU.add).then_inc(mg_made, 1)
                    until(base + 2 * (23 + n) + 2 + H)
                    for m in range(2):
                        kk = 4 * n + 2 * m
                        dve.wait_ge(mg_h, 4 * l + 2 * n + m + 1)
                        nc.vector.tensor_tensor(xt_lo[:, kk:kk + 2, :], gate[:, 1, kk:kk + 2, :],
                                                xt_hi[:, kk:kk + 2, :].bitcast(F32), ALU.subtract).then_inc(mg_l, 1)
                until(base + MIX_PIECES)

                def add_mixer(p, l=l):
                    t, half = p // 2, p % 2
                    if t == 0:
                        dve.wait_ge(y_full, 3 * l + 1)
                    else:
                        dve.wait_ge(piece_used, MIX_BASE[l] + MIX_PIECES - 2 + 2 * half)
                    residual_add(p, bank[UNIT[f"wo{2 * half + t}"] % 4], 2 * l + 1)

                norm(2 * l + 1, add_mixer, lambda: until(MIX_BASE[l] + MIX_PIECES + 1))
                norm_transposed(2 * l + 1, (0, 1))
                until(base + MIX_PIECES + 2)
                norm_transposed(2 * l + 1, (2, 3))
                until(base + MIX_PIECES + H)

                if l == 0:
                    def hidden(count, s, used):
                        dve.wait_ge(sg_done, count)
                        dve.wait_ge(piece_used, used)
                        nc.vector.tensor_tensor(hf[:, s, :], sg[:, :], bank[1][:, :], ALU.mult).then_inc(hf_done, 1)
                        dve.wait_ge(fh_h, count)
                        nc.vector.tensor_tensor(fh_lo[:, s, :, :], hf[:, s, :].rearrange("p (k t) -> p k t", k=2),
                                                fh_hi[:, s, :, :].bitcast(F32), ALU.subtract).then_inc(fh_l, 1)

                    dve.wait_ge(wr_h, 1)
                    nc.vector.tensor_tensor(wr_lo[:, :, :], wr_raw[:, :, :], wr_hi[:, :, :].bitcast(F32), ALU.subtract
                                            ).then_inc(wr_l, 1)
                    q0 = FFN_BASE
                    until(q0 + 4 + H)
                    hidden(1, 0, q0 + 4)
                    with dve.Fori(0, (STEPS - 1) // 2) as r:
                        for s in range(2):
                            q = q0 + 4 + 6 * s + H
                            for n in range(4):
                                split(q + n, done=12 * r + q + n + 1)
                            hidden(2 * r + s + 2, 1 - s, 12 * r + q0 + 8 + 6 * s)
                            for n in range(4, 6):
                                split(q + n, done=12 * r + q + n + 1)
                    cur[0] = q0 + 4 + 6 * (STEPS - 1) + H
                    until(q0 + FFN_PIECES + 2)

            nc.vector.memset(keys[:, :, :], 0.0)
            nc.vector.memset(gates[:, :, :], 0.0)
            step(nc.vector.memset(perm_t.bitcast(F32), 0.0))

            def r2(at):
                return rt[:, at:at + TB]

            def r8(at):
                return rt[:, at:at + TB * NE].rearrange("p (b e) -> p b e", b=TB)

            lg, one1, one2, tmp = r8(0), r8(16), r8(32), r8(48)
            m1, m2, k1, pex, dif, p1, p2 = r2(68), r2(70), r2(72), r2(64), r2(66), r2(74), r2(76)
            mask, over, run, cnt = r8(80), rt[:, 96:104], rt[:, 104:112], rt[:, 112:120]
            sel = rt[:, 120:120 + EXTRA * NE].rearrange("p (n e) -> p n e", n=EXTRA)
            fitems = rt[:, 160:160 + 1 + MAX_ITEMS]
            prod = rt[:, 176:176 + 5 * EXTRA * NE].rearrange("p (m n e) -> p m n e", m=5, n=EXTRA)
            rev = const[:, K_REV:K_REV + NE]
            dve.wait_ge(lg_full, 1)
            step(nc.vector.tensor_copy(lg, bank[4][:, 0:TB * NE].rearrange("p (b e) -> p b e", b=TB)))

            def pick(logits, best, one):
                step(nc.vector.tensor_reduce(best, logits, AX.X, ALU.max))
                for t in range(TB):
                    ins = nc.vector.scalar_tensor_tensor(out=tmp[:, t, :], in0=logits[:, t, :], scalar=best[:, t:t + 1],
                                                         in1=rev, op0=ALU.is_equal, op1=ALU.mult)
                step(ins)
                step(nc.vector.tensor_reduce(k1, tmp, AX.X, ALU.max))
                for t in range(TB):
                    ins = nc.vector.tensor_scalar(one[:, t, :], rev, k1[:, t:t + 1], None, ALU.is_equal)
                step(ins)

            pick(lg, m1, one1)
            step(nc.vector.scalar_tensor_tensor(out=lg, in0=one1, scalar=-3.0e38, in1=lg, op0=ALU.mult, op1=ALU.add))
            pick(lg, m2, one2)
            nc.vector.tensor_tensor(dif, m2, m1, ALU.subtract).then_inc(dif_done, 1)
            nc.vector.tensor_tensor(mask, one1, one2, ALU.add).then_inc(mask_done, 1)
            dve.wait_ge(hn_h, 1)
            nc.vector.tensor_tensor(hn_lo[:, :, :], hn[:, :, :], hn_hi[:, :, :].bitcast(F32), ALU.subtract
                                    ).then_inc(hn_l, 1)
            dve.wait_ge(rank_full, 1)
            step(nc.vector.tensor_copy(cnt, bank[5][:, TB * NE:TB * NE + NE]))
            nc.vector.scalar_tensor_tensor(out=keys[:, :, 0:NE],
                                           in0=bank[5][:, 0:TB * NE].rearrange("p (b e) -> p b e", b=TB),
                                           scalar=1.0, in1=mask, op0=ALU.add, op1=ALU.mult).then_inc(rank_read, 1)
            dve.wait_ge(rank_read, 1)

            def make_perm(i):
                for t in range(TB):
                    ins = nc.vector.tensor_scalar(perm[:, t, :], const[:, K_IOTA:K_IOTA + SLOTS],
                                                  keys[:, t, i], None, ALU.is_equal)
                ins.then_inc(perm_done, 1)

            make_perm(slice(0, 1))
            dve.wait_ge(pex_done, 1)
            step(nc.vector.tensor_scalar(p1, pex, 1.0, None, ALU.add))
            step(nc.vector.reciprocal(p1, p1))
            step(nc.vector.tensor_tensor(p2, pex, p1, ALU.mult))
            for t in range(TB):
                ins = nc.vector.tensor_scalar(gates[:, t, 1:1 + NE], one1[:, t, :], p1[:, t:t + 1], None, ALU.mult)
            step(ins)
            for t in range(TB):
                ins = nc.vector.scalar_tensor_tensor(out=gates[:, t, 1:1 + NE], in0=one2[:, t, :], scalar=p2[:, t:t + 1],
                                                     in1=gates[:, t, 1:1 + NE], op0=ALU.mult, op1=ALU.add)
            step(ins)
            step(nc.vector.tensor_scalar(over, cnt, float(SLOTS), None, ALU.is_gt))
            step(nc.vector.tensor_tensor_scan(run, const[:, K_ONE:K_ONE + NE], over, 0.0, ALU.mult, ALU.add))
            nc.vector.tensor_copy(fitems[:, 1:1 + NE], const[:, K_EID:K_EID + NE])
            nc.vector.tensor_scalar(fitems[:, 0:1], run[:, NE - 1:NE], float(NE), None, ALU.add)
            for n in range(EXTRA):
                ins = nc.vector.scalar_tensor_tensor(out=sel[:, n, :], in0=run, scalar=float(n + 1), in1=over,
                                                     op0=ALU.is_equal, op1=ALU.mult)
            step(ins)
            picked = [(keys[:, t, 0:NE], keys[:, t, NE:NE + EXTRA]) for t in range(TB)]
            picked += [(gates[:, t, 1:1 + NE], gates[:, t, 1 + NE:1 + NE + EXTRA]) for t in range(TB)]
            picked += [(const[:, K_EID:K_EID + NE], fitems[:, 1 + NE:1 + NE + EXTRA])]
            for n, (src, _) in enumerate(picked):
                ins = nc.vector.tensor_tensor(prod[:, n, :, :], sel, src.unsqueeze(1).to_broadcast([P, EXTRA, NE]), ALU.mult)
            step(ins)
            for n, (_, dst) in enumerate(picked):
                ins = nc.vector.tensor_reduce(dst, prod[:, n, :, :], AX.X, ALU.add)
            step(ins)
            step(nc.vector.tensor_scalar(keys[:, :, NE:NE + EXTRA], keys[:, :, NE:NE + EXTRA], -float(SLOTS), None, ALU.add))
            nc.vector.tensor_copy(items[:, :], fitems).then_inc(routed, 1)

            def gather_copies(count):
                for m in range(2):
                    dve.wait_ge(gather_full, count + m)
                    nc.vector.tensor_copy(ex_lo[:, 4 * m:4 * m + 4, :],
                                          bank[GATHER[2 + m]][:, :].rearrange("p (k s) -> p k s", k=4)).then_inc(gl_done, 1)

            def output_split(count):
                for m in range(2):
                    dve.wait_ge(ey_h, count + m + 1)
                    nc.vector.tensor_tensor(ys_lo[:, 512 * m:512 * m + 512], bank[4 + m][:, :],
                                            ys_hi[:, 512 * m:512 * m + 512].bitcast(F32), ALU.subtract).then_inc(ey_l, 1)

            def residual(n, count, i):
                t, half = n // 2, n % 2
                cols = slice(512 * half, 512 * half + 512)
                dve.wait_ge(scat_full, count + n + 1)
                nc.vector.scalar_tensor_tensor(out=x[:, t, cols], in0=bank[6 + n % 2][:, :], scalar=gates[:, t, i],
                                               in1=x[:, t, cols], op0=ALU.mult, op1=ALU.add).then_inc(scat_done, 1)

            gather_copies(3)
            dve.wait_ge(routed, 1)
            n_items = dve.value_load(items[0:1, 0:1], min_val=NE, max_val=MAX_ITEMS)
            q0 = MOE_BASE
            with dve.Fori(0, n_items) as i:
                def item_split(lo, hi, r=None):
                    for n in range(lo, hi):
                        done = ITEM_PIECES * i + q0 + n + 1
                        if r is not None:
                            done = done + 12 * r
                        half = ring_half(n // 2, i, 0 if r is None else r)
                        split(q0 + n, done=done, slot=half * R + (q0 + n) // 2 % R)

                with dve.If(i > 0):
                    item_split(0, H)
                output_split(2 * i)
                item_split(4, 8)
                for n in range(2):
                    residual(n, 4 * i, bass.ds(i, 1))
                item_split(8, 10)
                for n in range(2, 4):
                    residual(n, 4 * i, bass.ds(i, 1))
                item_split(10, 12)

                def hidden(count, used):
                    dve.wait_ge(esg_done, count)
                    dve.wait_ge(piece_used, used)
                    nc.vector.tensor_tensor(hf[:, 0, :], sg[:, :], bank[1][:, :], ALU.mult).then_inc(ehf_done, 1)

                def hidden_lo(count):
                    dve.wait_ge(eh_h, count)
                    nc.vector.tensor_tensor(eh_lo[:, :, :], bank[6][:, :].rearrange("p (k s) -> p k s", k=4),
                                            eh_hi[:, :, :].bitcast(F32), ALU.subtract).then_inc(eh_l, 1)

                hidden(ESTEPS * i + 1, ITEM_PIECES * i + q0 + 8)
                dve.wait_ge(pt_full, i + 1)
                make_perm(bass.ds(i + 1, 1))
                with dve.Fori(0, ESTEPS - 1) as r:
                    item_split(12, 14, r)
                    hidden_lo(ESTEPS * i + r + 1)
                    item_split(14, 20, r)
                    hidden(ESTEPS * i + r + 2, ITEM_PIECES * i + 12 * r + q0 + 16)
                    item_split(20, 24, r)
                hidden_lo(ESTEPS * i + ESTEPS)
                gather_copies(4 * i + 7)
            output_split(2 * n_items)
            norm(4, lambda p: residual(p, 4 * n_items, bass.ds(n_items, 1)))

        @block.gpsimd
        def _(pool):
            chain = [0]

            def step(ins):
                chain[0] += 1
                ins.then_inc(pool_step, 1)
                pool.wait_ge(pool_step, chain[0])

            def root(n):
                for t in range(TB):
                    pool.wait_ge(ms_done, 2 * n + t + 1)
                    nc.gpsimd.tensor_tensor(rs[:, t:t + 1], ms[:, t:t + 1], const[:, K_PW:K_PW + 1], ALU.pow
                                            ).then_inc(rs_done, 1)

            pool.wait_ge(base_in, 16)
            for l in range(DEPTH):
                root(2 * l)
                for h in range(HP):
                    pool.wait_ge(b_done, l + 1)
                    b_h = bb[:, h, :]
                    for n, m in enumerate(LEVELS):
                        blk = b_h.rearrange("p (a s m) -> p a s m", s=2, m=m)
                        dst = ex[:, n, :].rearrange("p (a s m) -> p a s m", s=2, m=m)
                        mid = blk[:, :, 0, m - 1:m].to_broadcast([P, SEQ // (2 * m), m])
                        nc.gpsimd.tensor_tensor(dst[:, :, 0, :], mid, blk[:, :, 0, :], ALU.subtract)
                        nc.gpsimd.tensor_tensor(dst[:, :, 1, :], blk[:, :, 1, :], mid, ALU.subtract)
                    blk = b_h.rearrange("p (c m) -> p c m", m=L)
                    nc.gpsimd.tensor_tensor(ex[:, NL, :].rearrange("p (c m) -> p c m", m=L),
                                            blk[:, :, L - 1:L].to_broadcast([P, NCH, L]), blk, ALU.subtract
                                            ).then_inc(expo_done, 1)
                    pool.wait_ge(exp_done, HP * l + h + 1)
                    if h == 0:
                        pool.wait_ge(q_done, l + 1)
                        pool.wait_ge(k_done, l + 1)
                        if l:
                            pool.wait_ge(o_full, TB * l)
                    nc.gpsimd.tensor_tensor(kdT[:, h, :], kT[:, h, :], ex[:, NL, :], ALU.mult).then_inc(kd_made, 1)
                    if h == 0:
                        pool.wait_ge(eb_done, l + 1)
                        nc.gpsimd.tensor_tensor(qiT[:, :, :], qT[:, :, :], eb[:, :, :], ALU.mult).then_inc(qi_done, 1)
                    if h:
                        pool.wait_ge(sc_full, 4 * l + 2)
                    for n in range(NL):
                        nc.gpsimd.tensor_tensor(qe[:, n, :], qT[:, h, :], ex[:, n, :], ALU.mult)
                        ins = nc.gpsimd.tensor_tensor(ke[:, n, :], kT[:, h, :], ex[:, n, :], ALU.mult)
                    ins.then_inc(qk_done, 1)
                    pool.wait_ge(qk_done, HP * l + h + 1)
                pool.wait_ge(silu_done, 2 * l + 2)
                if l == 0:
                    pool.wait_ge(params_in, 80)
                for t in range(TB):
                    g4 = gs[:, t, :].rearrange("p (h n) -> p h n", h=HEADS)
                    ins = nc.gpsimd.tensor_tensor(g4, g4, glag[:, l, :].unsqueeze(1).to_broadcast([P, HEADS, DV]), ALU.mult)
                ins.then_inc(gs_done, 1)
                for t in range(TB):
                    pool.wait_ge(oms_done, TB * l + t + 1)
                    nc.gpsimd.tensor_tensor(ors[:, t, :], oss[:, t, :], const[:, K_PW:K_PW + HEADS], ALU.pow
                                            ).then_inc(ors_done, 1)
                root(2 * l + 1)
            root(2 * DEPTH)

        @block.tensor
        def _(pe):
            def mm(out, lhs, rhs, first=False, last=False):
                return nc.tensor.matmul(out, lhs, rhs, start=first, stop=last, skip_group_check=True)

            def mm3(out, sta, mov, first=False, last=False):
                mm(out, sta[0], mov[0], first)
                mm(out, sta[0], mov[1])
                return mm(out, sta[1], mov[0], False, last)

            def piece(q, done=None):
                pe.wait_ge(lo_done, q + 1 if done is None else done)
                return w_hi[:, q % H, :], w_lo[:, q % H, :]

            def pair(p, f):
                return f(p[0]), f(p[1])

            def claim(l, name):
                n = UNIT[name]
                if n >= 4:
                    pe.wait_ge(*unit_read(l, UNIT_NAMES[n - 4]))
                else:
                    pe.wait_ge(tl_done, 8 * l + n + 1)
                return bank[n % 4]

            def norm_transposed(n):
                for t in range(TB):
                    for m in range(4):
                        if m % 2 == 0:
                            pe.wait_ge(hn_done, 4 * n + 2 * t + m // 2 + 1)
                        for k in range(2):
                            kk = 2 * m + k
                            ins = nc.tensor.transpose(bank[4 * (n % 2) + m][:, (2 * k + t) * P:(2 * k + t + 1) * P],
                                                      hn[:, t, kk * P:(kk + 1) * P], ident)
                        if t == TB - 1:
                            ins.then_inc(turned, 1)

            def channels(out, q0, blocks=2, counts=(None, None), ready=None):
                for half in range(2):
                    w = piece(q0 + half, counts[half])
                    w = pair(w, lambda a: a.rearrange("p (k n) -> p k n", k=4))
                    for k in range(4):
                        kk = 4 * half + k
                        if ready is not None and kk % 2 == 0:
                            pe.wait_ge(tl_done, ready + kk // 2 + 1)
                        for b in range(blocks):
                            ins = mm3(out[:, b * SEQ:(b + 1) * SEQ],
                                      pair(w, lambda a: a[:, k, b * P:(b + 1) * P]),
                                      (xt_hi[:, kk, :], xt_lo[:, kk, :]),
                                      kk == 0 and b == 0, kk == KT - 1 and b == blocks - 1)
                    ins.then_inc(piece_used, 1)

            def tokens(out, q0):
                for half in range(2):
                    w = pair(piece(q0 + half), lambda a: a.rearrange("p (k n) -> p k n", k=4))
                    for k in range(4):
                        kk = 4 * half + k
                        for t in range(TB):
                            ins = mm3(out[:, t * 256:(t + 1) * 256],
                                      (xt_hi[:, kk, t * P:(t + 1) * P], xt_lo[:, kk, t * P:(t + 1) * P]),
                                      pair(w, lambda a: a[:, k, :]), kk == 0 and t == 0, kk == KT - 1 and t == TB - 1)
                    ins.then_inc(piece_used, 1)

            pe.wait_ge(base_in, 16)
            for l in range(DEPTH):
                base = MIX_BASE[l]
                norm_transposed(2 * l)
                out = claim(l, "alow")
                channels(out, base, 1, ready=8 * l)

                def win(n, base=base, l=l):
                    name = WIN[n][0]
                    out = claim(l, name)
                    f = tokens if name[:2] in ("v0", "v1", "go") else channels
                    f(out, base + 2 + 2 * n)

                win(0)
                pe.wait_ge(al_done, l + 1)
                if l == 0:
                    pe.wait_ge(params_in, 80)
                else:
                    pe.wait_ge(sc_done, 4 * l)
                for h in range(HP):
                    ins = nc.tensor.matmul(bank[4][:, h * SEQ:(h + 1) * SEQ], wa2[:, l, h * P:(h + 1) * P],
                                           al[0:RANK, :], start=True, stop=True)
                ins.then_inc(z_full, 1)
                for n in range(1, 10):
                    win(n)
                def scores(batch):
                    h, first = batch // 2, 4 * (batch % 2)
                    if batch == 0:
                        pe.wait_ge(z_read, l + 1)
                    if 4 * l + batch:
                        pe.wait_ge(sc_done, 4 * l + batch)
                    pe.wait_ge(qk_done, HP * l + h + 1)
                    for m in range(first, min(first + 4, NL + 1)):
                        for c in range(NCH):
                            for a in range(2):
                                rows = slice(a * DK, (a + 1) * DK)
                                cols = slice(c * L, (c + 1) * L)
                                if m < NL:
                                    lhs, rhs = ke[rows, m, cols], qe[rows, m, cols]
                                else:
                                    lhs, rhs = kT[rows, h, cols], qT[rows, h, cols]
                                at = ((m - first) * TB + c // 2) * L
                                ins = nc.tensor.matmul(bank[4 + a][(c % 2) * L:(c % 2 + 1) * L, at:at + L], lhs, rhs,
                                                       start=True, stop=True)
                    ins.then_inc(sc_full, 1)

                win(10)
                for n in (11, 12, 13):
                    win(n)
                    if n != 12:
                        scores((n - 11) // 2)
                    if n == 12:
                        pe.wait_ge(kd_made, HP * l + HP)
                        pe.wait_ge(ya_l, l + 1)
                        if l:
                            pe.wait_ge(yb_done, TB * l)
                        for t in range(TB):
                            for h in range(HP):
                                at = (t * HP + h) * P
                                ins = nc.tensor.transpose(bank[7][:, at:at + P], kdT[:, h, t * P:(t + 1) * P], ident)
                        ins.then_inc(kdt_full, 1)
                pe.wait_ge(kdt_done, l + 1)
                pe.wait_ge(v_done, 2 * l + 2)
                for h in range(HP):
                    for c in range(NCH - 1):
                        for a in range(2):
                            rows = slice((c % 2) * L, (c % 2 + 1) * L)
                            head = 2 * h + a
                            at = (c // 2 * 2 + h) * DV
                            ins = nc.tensor.matmul(bank[6 + c % 2][a * DK:(a + 1) * DK, at:at + DV],
                                                   kd[rows, c // 2, h, a * DK:(a + 1) * DK],
                                                   v[rows, c // 2, head * DV:(head + 1) * DV], start=True, stop=True)
                ins.then_inc(inc_full, 1)
                win(14)
                for n in (15, 16, 17, 18):
                    win(n)
                    if n % 2 == 0:
                        scores(n // 2 - 6)
                win(19)
                pe.wait_ge(sc_done, 4 * (l + 1))
                pe.wait_ge(st_done, l + 1)
                pe.wait_ge(qi_done, l + 1)
                for t in range(TB):
                    for head in range(HEADS):
                        for c in range(2):
                            rows = slice(c * L, (c + 1) * L)
                            cols = slice(head * DV, (head + 1) * DV)
                            ins = mm(bank[6 + t][rows, cols], sc[rows, t, head, :], v[rows, t, cols], head == 0)
                ins.then_inc(o_part, 1)
                for a in range(2):
                    pe.wait_ge(o_part, 2 * l + a + 1)
                    krows = slice(a * DK, (a + 1) * DK)
                    for t in range(TB):
                        for h in range(HP):
                            for c in (2 * t, 2 * t + 1):
                                if c:
                                    head = 2 * h + a
                                    ins = mm(bank[6 + t][(c % 2) * L:(c % 2 + 1) * L, head * DV:(head + 1) * DV],
                                             qiT[krows, h, c * L:(c + 1) * L], st[krows, c - 1, h, :], False, a == 1)
                        if a == 1:
                            ins.then_inc(o_full, 1)
                    if a == 0:
                        ins.then_inc(o_part, 1)

                def branch(q0, y, first, names, l=l):
                    outs = [claim(l, name) for name in names]
                    for half in range(2):
                        w = pair(piece(q0 + half), lambda a: a.rearrange("p (k n) -> p k n", k=2))
                        for k in range(2):
                            kk = 2 * half + k
                            if first is not None and k == 0:
                                pe.wait_ge(yt_l, first + half + 1)
                            for b in range(4):
                                ins = mm3(outs[b // 2][:, b % 2 * SEQ:(b % 2 + 1) * SEQ],
                                          pair(w, lambda a: a[:, k, b * P:(b + 1) * P]),
                                          (y[0][:, kk, :], y[1][:, kk, :]), kk == 0 and b % 2 == 0,
                                          kk == CB - 1 and b % 2 == 1)
                        ins.then_inc(piece_used, 1)

                pe.wait_ge(ya_l, l + 1)
                q = base + 2 * (1 + len(WIN))
                branch(q, (ya_hi, ya_lo), None, ("ya0", "ya1"))

                def y_transposed(l=l):
                    for n in range(2):
                        for t in range(TB):
                            pe.wait_ge(yb_done, TB * l + t + 1)
                        for k in range(2):
                            for t in range(TB):
                                kk = 2 * n + k
                                ins = nc.tensor.transpose(bank[4 + n][:, (2 * k + t) * P:(2 * k + t + 1) * P],
                                                          yb[:, t, kk * P:(kk + 1) * P], ident)
                        ins.then_inc(turned, 1)

                y_transposed()
                branch(q + 2, (ya_hi, ya_lo), None, ("ya2", "ya3"))
                branch(q + 4, (yb_hi, yb_lo), 2 * l, ("yb0", "yb1"))
                branch(q + 6, (yb_hi, yb_lo), 2 * l, ("yb2", "yb3"))
                q += 8
                outs = {}

                def out_piece(kh, half, s, t, l=l, q=q):
                    w = pair(piece(q + 4 * kh + 2 * half + s), lambda a: a.rearrange("p (k n) -> p k n", k=2))
                    pe.wait_ge(mg_l, 4 * l + 2 * kh + s + 1)
                    for k in range(2):
                        kk = 4 * kh + 2 * s + k
                        ins = mm3(outs[2 * half + t][:, :],
                                  (xt_hi[:, kk, t * P:(t + 1) * P], xt_lo[:, kk, t * P:(t + 1) * P]),
                                  pair(w, lambda a: a[:, k, :]), kk == 0, kk == KT - 1)
                    return ins

                for half in range(2):
                    for t in range(TB):
                        outs[2 * half + t] = claim(l, f"wo{2 * half + t}")
                    for s in range(2):
                        for t in range(TB):
                            ins = out_piece(0, half, s, t)
                        ins.then_inc(piece_used, 1)
                for t in range(TB):
                    for half in range(2):
                        for s in range(2):
                            ins = out_piece(1, half, s, t)
                            if t == TB - 1:
                                ins.then_inc(piece_used, 1)
                    if t == 0:
                        ins.then_inc(y_full, 1)
                norm_transposed(2 * l + 1)

                if l == 0:
                    q0 = FFN_BASE

                    def up(q, counts, free, ready=None):
                        if free is not None:
                            pe.wait_ge(sg_done, free)
                        channels(bank[0], q, counts=counts[0:2], ready=ready)
                        if free is not None:
                            pe.wait_ge(hf_done, free)
                        channels(bank[1], q + 2, counts=counts[2:4])

                    def down_part(w, s, k, t, half, last=False):
                        return mm3(bank[4 + 2 * t + half][:, :],
                                   (fh_hi[:, s, k, t * P:(t + 1) * P], fh_lo[:, s, k, t * P:(t + 1) * P]),
                                   pair(w, lambda a: a[:, 512 * half:512 * half + 512]), False, last)

                    def down(q, s, counts, count):
                        pe.wait_ge(fh_l, count)
                        for k in range(2):
                            w = piece(q + k, done=counts[k])
                            for t in range(TB):
                                for half in range(2):
                                    ins = down_part(w, s, k, t, half)
                            ins.then_inc(piece_used, 1)

                    up(q0, (None,) * 4, None, ready=4)
                    pe.wait_ge(init_done, 1)
                    pe.wait_ge(tl_done, 8)
                    for n in range(4):
                        mm(bank[4 + n][:, :], zeros[:, 0:P], zeros[:, :], True)
                    with pe.Fori(0, (STEPS - 1) // 2) as r:
                        for s in range(2):
                            q = q0 + 4 + 6 * s
                            counts = [12 * r + q + n + 1 for n in range(6)]
                            up(q, counts, 2 * r + s + 1)
                            down(q + 4, s, counts[4:], 2 * r + s + 1)
                    pe.wait_ge(fh_l, STEPS)
                    w = [piece(q0 + FFN_PIECES - 2 + k) for k in range(2)]
                    for t in range(TB):
                        for half in range(2):
                            for k in range(2):
                                ins = down_part(w[k], 0, k, t, half, k == 1)
                                if (t, half) == (1, 1):
                                    ins.then_inc(piece_used, 1)
                            if (t, half) in ((0, 1), (1, 0)):
                                ins.then_inc(y_full, 1)

            pe.wait_ge(wr_l, 1)
            pe.wait_ge(tl_done, 16)
            for t in range(TB):
                for k in range(KT):
                    ins = mm3(bank[4][:, t * NE:(t + 1) * NE],
                              (xt_hi[:, k, t * P:(t + 1) * P], xt_lo[:, k, t * P:(t + 1) * P]),
                              (wr_hi[:, k, :], wr_lo[:, k, :]), k == 0 and t == 0, k == KT - 1 and t == TB - 1)
            ins.then_inc(lg_full, 1)
            pe.wait_ge(mask_done, 1)
            masks = rt[:, 80:96].rearrange("p (b e) -> p b e", b=TB)
            tri = const[:, K_TRI:K_TRI + P]
            nc.tensor.matmul(bank[5][:, 0:NE], tri, masks[:, 0, :], start=True, stop=True)
            nc.tensor.matmul(bank[5][:, NE:2 * NE], tri, masks[:, 1, :], start=True, stop=False)
            nc.tensor.matmul(bank[5][:, NE:2 * NE], ones, masks[:, 0, :], start=False, stop=True)
            nc.tensor.matmul(bank[5][:, 2 * NE:3 * NE], ones, masks[:, 0, :], start=True, stop=False)
            nc.tensor.matmul(bank[5][:, 2 * NE:3 * NE], ones, masks[:, 1, :], start=False, stop=True
                             ).then_inc(rank_full, 1)

            def gather(m, src):
                for d in range(4):
                    dd = 4 * (m % 2) + d
                    for t in range(TB):
                        ins = mm(bank[GATHER[m]][:, d * SLOTS:(d + 1) * SLOTS], src[:, t, dd * P:(dd + 1) * P],
                                 perm[:, t, :], d == 0 and t == 0, d == 3 and t == TB - 1)
                ins.then_inc(gather_full, 1)

            def clear_output():
                for m in range(2):
                    ins = mm(bank[4 + m][:, :], zeros[:, 0:P], zeros[:, :], True)
                return ins

            def scatter(first, i, lo_count):
                for n in (first, first + 1):
                    t, half = n // 2, n % 2
                    if n < 2:
                        pe.wait_ge(ey_l, lo_count + n + 1)
                    if n == 0:
                        pe.wait_ge(gl_done, 2 * i + 2)
                    if n >= 2:
                        pe.wait_ge(scat_done, 4 * i + n - 1)
                    cols = slice(512 * half, 512 * half + 512)
                    lhs = perm_t[:, t * P:(t + 1) * P]
                    mm(bank[6 + n % 2][:, :], lhs, ys_hi[:, cols], True)
                    mm(bank[6 + n % 2][:, :], lhs, ys_lo[:, cols], False, True).then_inc(scat_full, 1)

            pe.wait_ge(rank_full, 1)
            pe.wait_ge(rank_read, 1)
            clear_output().then_inc(cleared, 1)
            pe.wait_ge(perm_done, 1)
            pe.wait_ge(hn_l, 1)
            gather(0, hn_hi)
            gather(1, hn_hi)
            gather(2, hn_lo)
            pe.wait_ge(gh_done, 1)
            gather(3, hn_lo)
            pe.wait_ge(routed, 1)
            n_items = pe.value_load(items[0:1, 0:1], min_val=NE, max_val=MAX_ITEMS)
            q0 = MOE_BASE
            with pe.Fori(0, n_items) as i:
                def done(n, r=None):
                    d = ITEM_PIECES * i + q0 + n + 1
                    return d if r is None else d + 12 * r

                def expert_up(out, n0, halves, r=None):
                    for s in halves:
                        w = pair(piece(q0 + n0 + s, done=done(n0 + s, r)), lambda a: a.rearrange("p (k n) -> p k n", k=2))
                        for k in range(2):
                            kk = 2 * s + k
                            ins = mm3(out[:, :], (ex_hi[:, kk, :], ex_lo[:, kk, :]),
                                      pair(w, lambda a: a[:, k, :]), kk == 0, kk == KT - 1)
                        ins.then_inc(piece_used, 1)

                def transposes(count, free=None):
                    pe.wait_ge(ehf_done, count)
                    for k in range(4):
                        ins = nc.tensor.transpose(bank[6][:, k * P:(k + 1) * P], hf[:, 0, k * P:(k + 1) * P], ident)
                    ins.then_inc(t_full, 1)

                def expert_down(n0, count, halves, r=None):
                    for s in halves:
                        if s == 0:
                            pe.wait_ge(eh_l, count)
                        w = piece(q0 + n0 + s, done=done(n0 + s, r))
                        for half in range(2):
                            ins = mm3(bank[4 + half][:, :], (eh_hi[:, s, :], eh_lo[:, s, :]),
                                      pair(w, lambda a: a[:, 512 * half:512 * half + 512]), False, False)
                        ins.then_inc(piece_used, 1)

                pe.wait_ge(gl_done, 2 * i + 2)
                pe.wait_ge(gh_done, 2 * i + 2)
                expert_up(bank[0], 0, range(4))
                scatter(0, i, 2 * i)
                expert_up(bank[1], 4, range(2))
                scatter(2, i, 2 * i)
                expert_up(bank[1], 4, range(2, 4))
                pe.wait_ge(scat_done, 4 * i + 4)
                for t in range(TB):
                    ins = nc.tensor.transpose(bank[7][:, t * P:(t + 1) * P], perm[:, t, :].bitcast(F32), ident)
                ins.then_inc(pt_full, 1)
                clear_output()
                with pe.Fori(0, ESTEPS - 1) as r:
                    pe.wait_ge(esg_done, ESTEPS * i + r + 1)
                    expert_up(bank[0], 8, range(2), r)
                    transposes(ESTEPS * i + r + 1)
                    expert_up(bank[0], 8, range(2, 4), r)
                    expert_up(bank[1], 12, range(4), r)
                    expert_down(16, ESTEPS * i + r + 1, range(4), r)
                transposes(ESTEPS * i + ESTEPS)
                pe.wait_ge(perm_done, i + 2)
                pe.wait_ge(pt_done, i + 1)
                gather(0, hn_hi)
                pe.wait_ge(esg_done, ESTEPS * i + ESTEPS)
                gather(1, hn_hi)
                gather(2, hn_lo)
                expert_down(80, ESTEPS * i + ESTEPS, range(2))
                pe.wait_ge(gh_done, 2 * i + 3)
                gather(3, hn_lo)
                expert_down(80, ESTEPS * i + ESTEPS, range(2, 4))
            scatter(0, n_items, 2 * n_items)
            scatter(2, n_items, 2 * n_items)


def kernel(**inputs):
    import concourse.bacc as _bacc
    from concourse.bass_utils import run_bass_kernel_spmd as _run

    nc = _bacc.Bacc("TRN2", target_bir_lowering=False, num_devices=1, dynamic_dma_scratch_size=1024)
    a = {name: np.ascontiguousarray(value) for name, value in inputs.items()}
    taps = a["conv_w"].transpose(0, 2, 1).reshape(DEPTH, CB, P, TAPS).transpose(0, 2, 1, 3).reshape(DEPTH, P, CB * TAPS)
    bias = a["b_a"].reshape(DEPTH, HP, P).transpose(0, 2, 1)
    feed = [("x", a["x"]), ("ln1", a["ln1_g"]), ("w_in", a["w_in"]), ("w_a2", a["w_a2"]),
            ("small", np.ascontiguousarray(np.concatenate([taps, bias], axis=2))), ("gla_g", a["gla_norm_g"]),
            ("w_br", a["w_branch"]), ("w_out", a["w_out"]), ("ln2", a["ln2_g"]), ("fg", a["ffn_w_gate"]),
            ("fu", a["ffn_w_up"]), ("fd", a["ffn_w_down"]), ("w_r", a["w_router"]), ("eg", a["moe_w_gate"]),
            ("eu", a["moe_w_up"]), ("ed", a["moe_w_down"]), ("fin", a["final_g"]), ("const", constants())]
    arrays = {f"in_{name}_dram": value for name, value in feed}
    args = [nc.dram_tensor(name, value.shape, F32, kind="ExternalInput").ap() for name, value in arrays.items()]
    args.append(nc.dram_tensor("out_0_dram", (1, SEQ, D), F32, kind="ExternalOutput").ap())
    trunk(nc, *args)
    r = _run(nc, [arrays], core_ids=[0])
    return r.results[0]["out_0_dram"]
```
